# Optimizing a Trainium2 kernel written in Bass

```python
import jax, jax.numpy as jnp
from jax import lax
import numpy as np

D_MODEL = 1024
BATCH = 1
SEQ = 512
DEPTH = 2

N_MEM = 256
N_MIXERS = 2
EPS = 1e-6
CONV_KERNEL = 31
GLA_HEADS = 4
GLA_DK = D_MODEL // 2
GLA_DV = D_MODEL
GLA_DKH = GLA_DK // GLA_HEADS
GLA_DVH = GLA_DV // GLA_HEADS
GLA_RANK = 16
GLA_TAU = 16.0
GLA_CHUNK = 64
XATTN_HEADS = 4
XATTN_HD = D_MODEL // XATTN_HEADS
N_GROUPS = 4
EXPERTS_PER_GROUP = 8
N_EXPERTS = N_GROUPS * EXPERTS_PER_GROUP
TOP_K = 2
D_EXPERT = D_MODEL // 2
MOE_BLOCK = 128

kernel_name = 'hybrid_conv_gla_memxattn_hmoe'

def rms_norm(x, g):
    xf = x.astype(jnp.float32)
    y = xf * lax.rsqrt(jnp.mean(xf * xf, axis=-1, keepdims=True) + EPS)
    return (y * g.astype(jnp.float32)).astype(x.dtype)

def conformer_conv(h, w_in, b_in, w_dw, b_dw, ln_g, ln_b, w_out, b_out):
    u = h @ w_in + b_in
    a, gt = jnp.split(u, 2, axis=-1)
    u = a * jax.nn.sigmoid(gt)
    u = lax.conv_general_dilated(
        u, w_dw[:, None, :], window_strides=(1,), padding=[(CONV_KERNEL - 1, 0)],
        dimension_numbers=('NWC', 'WIO', 'NWC'), feature_group_count=D_MODEL) + b_dw
    uf = u.astype(jnp.float32)
    mu = jnp.mean(uf, axis=-1, keepdims=True)
    var = jnp.mean(jnp.square(uf - mu), axis=-1, keepdims=True)
    un = ((uf - mu) * lax.rsqrt(var + EPS) * ln_g.astype(jnp.float32) + ln_b.astype(jnp.float32)).astype(h.dtype)
    return jax.nn.silu(un) @ w_out + b_out

def gla_mixer(h, w_in, w_a2, b_a, norm_g, w_o):
    B, S, _ = h.shape
    n_chunks = S // GLA_CHUNK
    proj = h @ w_in
    q, k, v, a_lr, r = jnp.split(
        proj, [GLA_DK, 2 * GLA_DK, 2 * GLA_DK + GLA_DV, 2 * GLA_DK + GLA_DV + GLA_RANK], axis=-1)
    log_a = jax.nn.log_sigmoid((a_lr @ w_a2 + b_a).astype(jnp.float32)) / GLA_TAU

    def chunks(t, d):
        return t.astype(jnp.float32).reshape(B, n_chunks, GLA_CHUNK, GLA_HEADS, d).transpose(1, 0, 3, 2, 4)

    qc = chunks(q, GLA_DKH) * (GLA_DKH ** -0.5)
    kc = chunks(k, GLA_DKH)
    vc = chunks(v, GLA_DVH)
    bc = jnp.cumsum(chunks(log_a, GLA_DKH), axis=3)
    causal = jnp.tril(jnp.ones((GLA_CHUNK, GLA_CHUNK), dtype=bool))[:, :, None]

    def step(state, inp):
        qi, ki, vi, bi = inp
        diff = bi[:, :, :, None, :] - bi[:, :, None, :, :]
        decay = jnp.exp(jnp.where(causal, diff, -jnp.inf))
        att = jnp.sum(qi[:, :, :, None, :] * ki[:, :, None, :, :] * decay, axis=-1)
        o = jnp.einsum('bhij,bhjv->bhiv', att, vi) + jnp.einsum('bhik,bhkv->bhiv', qi * jnp.exp(bi), state)
        b_last = bi[:, :, -1:, :]
        k_dec = ki * jnp.exp(b_last - bi)
        new_state = jnp.exp(b_last)[:, :, 0, :, None] * state + jnp.einsum('bhjk,bhjv->bhkv', k_dec, vi)
        return new_state, o

    state0 = jnp.zeros((B, GLA_HEADS, GLA_DKH, GLA_DVH), jnp.float32)
    _, o = lax.scan(step, state0, (qc, kc, vc, bc))
    o = o.transpose(1, 0, 3, 2, 4).reshape(B, S, GLA_HEADS, GLA_DVH)
    o = o * lax.rsqrt(jnp.mean(o * o, axis=-1, keepdims=True) + EPS) * norm_g.astype(jnp.float32)
    o = o.reshape(B, S, GLA_DV).astype(h.dtype) * jax.nn.silu(r)
    return o @ w_o

def mem_cross_attn(h, m, w_q, w_kv, w_o):
    B, S, _ = h.shape
    q = (h @ w_q).reshape(B, S, XATTN_HEADS, XATTN_HD)
    k, v = jnp.split(m @ w_kv, 2, axis=-1)
    k = k.reshape(B, N_MEM, XATTN_HEADS, XATTN_HD)
    v = v.reshape(B, N_MEM, XATTN_HEADS, XATTN_HD)
    s = jnp.einsum('bshd,bmhd->bhsm', q, k).astype(jnp.float32) * (XATTN_HD ** -0.5)
    p = jax.nn.softmax(s, axis=-1).astype(v.dtype)
    o = jnp.einsum('bhsm,bmhd->bshd', p, v).reshape(B, S, D_MODEL)
    return o @ w_o

def hier_moe(h, w_grp, b_grp, w_exp, b_exp, w_gate, w_up, w_down):
    B, S, D = h.shape
    T = B * S
    hf = h.reshape(T, D)
    gl = (hf @ w_grp + b_grp).astype(jnp.float32)
    pg = jax.nn.softmax(gl, axis=-1)
    g_sel = jnp.argmax(gl, axis=-1)
    pg_sel = jnp.take_along_axis(pg, g_sel[:, None], axis=1)
    el = (hf @ w_exp + b_exp).astype(jnp.float32).reshape(T, N_GROUPS, EXPERTS_PER_GROUP)
    el_sel = jnp.take_along_axis(el, g_sel[:, None, None], axis=1)[:, 0]
    pe = jax.nn.softmax(el_sel, axis=-1)
    top_p, top_i = lax.top_k(pe, TOP_K)
    gate = pg_sel * top_p / jnp.sum(top_p, axis=-1, keepdims=True)
    expert_id = g_sel[:, None].astype(jnp.int32) * EXPERTS_PER_GROUP + top_i.astype(jnp.int32)

    A = T * TOP_K
    e_flat = expert_id.reshape(A)
    g_flat = gate.reshape(A)
    order = jnp.argsort(e_flat)
    sorted_e = e_flat[order]
    token_idx = order // TOP_K
    counts = jnp.bincount(e_flat, length=N_EXPERTS)
    offsets = jnp.cumsum(counts) - counts
    padded = (counts + MOE_BLOCK - 1) // MOE_BLOCK * MOE_BLOCK
    pad_ends = jnp.cumsum(padded)
    pad_offsets = pad_ends - padded
    dest = pad_offsets[sorted_e] + jnp.arange(A) - offsets[sorted_e]
    n_blocks = -(-A // MOE_BLOCK) + N_EXPERTS
    x_buf = jnp.zeros((n_blocks * MOE_BLOCK, D), h.dtype).at[dest].set(hf[token_idx])
    block_expert = jnp.minimum(
        jnp.searchsorted(pad_ends, jnp.arange(n_blocks) * MOE_BLOCK, side='right'), N_EXPERTS - 1)

    def expert_block(args):
        xb, e = args
        return (jax.nn.silu(xb @ w_gate[e]) * (xb @ w_up[e])) @ w_down[e]

    y_buf = lax.map(expert_block, (x_buf.reshape(n_blocks, MOE_BLOCK, D), block_expert)).reshape(-1, D)
    y = y_buf[dest] * g_flat[order][:, None].astype(h.dtype)
    out = jnp.zeros((T, D), h.dtype).at[token_idx].add(y)
    return out.reshape(B, S, D)

def setup_inputs(seed: int = 0) -> dict:
    key = jax.random.key(seed)
    ks = iter(jax.random.split(key, 40))
    n_conv = (DEPTH + 1) // 2
    n_gla = DEPTH // 2
    D = D_MODEL

    def nrm(shape, scale):
        return jax.random.normal(next(ks), shape, jnp.float32) * scale

    def gain(shape):
        return 1.0 + 0.02 * jax.random.normal(next(ks), shape, jnp.float32)

    gla_in_cols = 2 * GLA_DK + GLA_DV + GLA_RANK + GLA_DV
    return {
        'x': nrm((BATCH, SEQ, D), 1.0),
        'mem': nrm((BATCH, N_MEM, D), 1.0),
        'norm_mix': gain((DEPTH, D)),
        'norm_xattn': gain((DEPTH, D)),
        'norm_ffn': gain((DEPTH, D)),
        'norm_mem': gain((D,)),
        'norm_final': gain((D,)),
        'conv_w_in': nrm((n_conv, D, 2 * D), D ** -0.5),
        'conv_b_in': nrm((n_conv, 2 * D), 0.02),
        'conv_w_dw': nrm((n_conv, CONV_KERNEL, D), CONV_KERNEL ** -0.5),
        'conv_b_dw': nrm((n_conv, D), 0.02),
        'conv_ln_g': gain((n_conv, D)),
        'conv_ln_b': nrm((n_conv, D), 0.02),
        'conv_w_out': nrm((n_conv, D, D), D ** -0.5),
        'conv_b_out': nrm((n_conv, D), 0.02),
        'gla_w_in': nrm((n_gla, D, gla_in_cols), D ** -0.5),
        'gla_w_a2': nrm((n_gla, GLA_RANK, GLA_DK), GLA_RANK ** -0.5),
        'gla_b_a': nrm((n_gla, GLA_DK), 0.1),
        'gla_norm_g': gain((n_gla, GLA_DVH)),
        'gla_w_o': nrm((n_gla, GLA_DV, D), GLA_DV ** -0.5),
        'xa_w_q': nrm((DEPTH, D, D), D ** -0.5),
        'xa_w_kv': nrm((DEPTH, D, 2 * D), D ** -0.5),
        'xa_w_o': nrm((DEPTH, D, D), D ** -0.5),
        'moe_w_grp': nrm((DEPTH, D, N_GROUPS), D ** -0.5),
        'moe_b_grp': nrm((DEPTH, N_GROUPS), 0.01),
        'moe_w_exp': nrm((DEPTH, D, N_EXPERTS), D ** -0.5),
        'moe_b_exp': nrm((DEPTH, N_EXPERTS), 0.01),
        'moe_w_gate': nrm((DEPTH, N_EXPERTS, D, D_EXPERT), D ** -0.5),
        'moe_w_up': nrm((DEPTH, N_EXPERTS, D, D_EXPERT), D ** -0.5),
        'moe_w_down': nrm((DEPTH, N_EXPERTS, D_EXPERT, D), D_EXPERT ** -0.5),
    }

def reference(x, mem, norm_mix, norm_xattn, norm_ffn, norm_mem, norm_final,
              conv_w_in, conv_b_in, conv_w_dw, conv_b_dw, conv_ln_g, conv_ln_b, conv_w_out, conv_b_out,
              gla_w_in, gla_w_a2, gla_b_a, gla_norm_g, gla_w_o,
              xa_w_q, xa_w_kv, xa_w_o,
              moe_w_grp, moe_b_grp, moe_w_exp, moe_b_exp, moe_w_gate, moe_w_up, moe_w_down):
    mem_n = rms_norm(mem, norm_mem)
    for i in range(DEPTH):
        h = rms_norm(x, norm_mix[i])
        j = i // N_MIXERS
        if i % N_MIXERS == 0:
            x = x + conformer_conv(h, conv_w_in[j], conv_b_in[j], conv_w_dw[j], conv_b_dw[j],
                                   conv_ln_g[j], conv_ln_b[j], conv_w_out[j], conv_b_out[j])
        else:
            x = x + gla_mixer(h, gla_w_in[j], gla_w_a2[j], gla_b_a[j], gla_norm_g[j], gla_w_o[j])
        x = x + mem_cross_attn(rms_norm(x, norm_xattn[i]), mem_n, xa_w_q[i], xa_w_kv[i], xa_w_o[i])
        x = x + hier_moe(rms_norm(x, norm_ffn[i]), moe_w_grp[i], moe_b_grp[i], moe_w_exp[i], moe_b_exp[i],
                         moe_w_gate[i], moe_w_up[i], moe_w_down[i])
    return rms_norm(x, norm_final)


_drawn_inputs = setup_inputs


def setup_inputs(seed=0):
    import zlib

    import numpy as np

    out = dict(_drawn_inputs(seed))
    spreads = {}
    factors = {'norm_xattn': 4.687,
     'norm_mem': 3.348,
     'norm_final': 2.74,
     'gla_norm_g': 3.019,
     'moe_b_grp': 2.995,
     'moe_b_exp': 3.776}
    for name, (base, spread) in spreads.items():
        noise = np.random.default_rng([zlib.crc32(name.encode()), seed]).standard_normal(out[name].shape)
        drawn = base * np.exp(spread * noise) if base else spread * noise
        out[name] = __import__('jax').numpy.asarray(drawn.astype(out[name].dtype))
    for name, factor in factors.items():
        out[name] = (out[name] * factor).astype(out[name].dtype)
    return out
```

```python
from contextlib import ExitStack

import concourse.bass as bass
from concourse import mybir

F32 = mybir.dt.float32
F32R = mybir.dt.float32r
I32 = mybir.dt.int32
U32 = mybir.dt.uint32
ALU = mybir.AluOpType
ACT = mybir.ActivationFunctionType
AX = mybir.AxisListType

P = 128
D = 1024
T = 512
DEPTH = 2
NMEM = 256
C = D // P
TT = T // P
EPS = 1e-6
KW = 31
PADW = T + KW - 1
HEADS = 4
DK = 128
CH = 64
NCH = T // CH
RANK = 16
TAU = 16.0
NG, EG = 4, 8
NE = NG * EG
FE = 512
FC = FE // P
SL = 64
ROUNDS = T // SL
PAIRS = NE // 2
RING = 6
BANK = 512
BIG = 1.0e30

VROWS = {}
_n = 0
for _name, _rows in (("norm_mix", 16), ("norm_xattn", 16), ("norm_ffn", 16), ("norm_final", 8), ("norm_mem", 8),
                     ("conv_b_in", 16), ("conv_b_dw", 8), ("conv_ln_g", 8), ("conv_ln_b", 8), ("conv_b_out", 8),
                     ("gla_b_a", 4), ("gla_norm_g", 2)):
    VROWS[_name] = (_n, _rows)
    _n += _rows
NVEC = _n
WDW_ROWS = KW * C // 2


class BankPlan:

    def __init__(self):
        self.uses = [0] * 8
        self.next = 0
        self.at = {}

    def use(self, key, bank=None):
        if bank is None:
            bank = self.next
            self.next = (self.next + 1) % 8
        self.at[key] = (bank, self.uses[bank])
        self.uses[bank] += 1
        return self.at[key]


def weight_tiles():
    conv = [("conv_in", 0), ("conv_in", 2), ("conv_in", 1), ("conv_in", 3)]
    kv = [("kv", i) for i in range(4)]
    tail = [("xq", 0), ("xq", 1), ("xo", 0), ("xo", 1)]
    layer0 = conv + kv + [("conv_out", 0), ("conv_out", 1)] + tail
    layer1 = [("gla_in", 0), ("gla_in", 1), ("gla_v", 0), ("gla_v", 1), ("gla_r", 0), ("gla_r", 1),
              ("gla_o", 0), ("gla_o", 1)] + kv + tail
    return [layer0, layer1]


def build(nc, a, out):
    plan = BankPlan()
    tiles = weight_tiles()
    tile_no = {}
    n = 0
    moe_base = []
    for l in range(DEPTH):
        for t in tiles[l]:
            tile_no[(l,) + t] = n
            n += 1
        moe_base.append(n)
        n += 3 * NE
    release = {}

    with ExitStack() as ctx:
        def sb(name, shape, dt=F32, where=ctx):
            return where.enter_context(nc.sbuf_tensor(name, shape, dt))

        def sem(name):
            return ctx.enter_context(nc.semaphore(name))

        ring = sb("ring", [P, RING, C * 512])
        xT = sb("xT", [P, C, T])
        hT = sb("hT", [P, C, T])
        ident = sb("ident", [P, P])
        ones = sb("ones", [P, P])
        tri = sb("tri", [P, P])
        gmask = sb("gmask", [P, P])
        vecT = sb("vecT", [P, NVEC])
        memT = sb("memT", [P, C, NMEM])
        iota = sb("iota", [P, SL])
        small = sb("small", [P, 160])
        dg = sb("dg", [P, TT, P])
        cnt_i = sb("cnt_i", [P, DEPTH], I32)
        rstat = small[:, 0:4]
        rrec = small[:, 4:8]
        mstat = small[:, 8:10]
        mrec = small[:, 10:12]
        nmax = small[:, 12:28]
        nmaxs = small[:, 28:44]
        ssum = small[:, 44:60]
        srec = small[:, 60:76]
        dec = small[:, 76:108]
        gslot = small[:, 108:109]
        gpair = small[:, 110:118]
        maxc = small[:, 118:119]
        musum = small[:, 119:123]

        with ExitStack() as s:
            RU = sb("RU", [P, C * PADW], where=s)
            RC = sb("RC", [P, C * T], where=s)
            RK = sb("RK", [P, C * T], where=s)
            R5 = sb("R5", [P, HEADS * T], where=s)
            SS = sb("SS", [P, 2, 256], where=s)
            EB = sb("EB", [P, 2, T], where=s)
            AT = sb("AT", [P, TT, P], where=s)
        with ExitStack() as s:
            hhi = sb("hhi", [P, TT, D], F32R, where=s)
            hlo = sb("hlo", [P, TT, D], F32R, where=s)
            yhi = sb("yhi", [P, D], F32R, where=s)
            ylo = sb("ylo", [P, D], F32R, where=s)
            onehot = sb("onehot", [P, TT, 2 * SL], F32R, where=s)
            onehotT = sb("onehotT", [P, T], F32R, where=s)
            identR = sb("identR", [P, P], F32R, where=s)
            ptab = sb("ptab", [P, ROUNDS * PAIRS, 2 * TT], where=s)
            gtab = sb("gtab", [P, ROUNDS * PAIRS, 2 * TT], where=s)
            wr = sb("wr", [P, C, NG + NE], where=s)
            brow = sb("brow", [1, NG + NE], where=s)
            lg = sb("lg", [P, TT, NG + NE], where=s)
            rt = sb("rt", [P, 640], where=s)
        u = RU[:, :].rearrange("p (c w) -> p c w", c=C)
        x_tm = RC[:, :].rearrange("p (t d) -> p t d", t=TT)
        cv = RC[:, :].rearrange("p (c t) -> p c t", c=C)
        mem_tm = RK[:, 0:2 * D].rearrange("p (t d) -> p t d", t=2)
        vrows = R5[:, 0:3 * P]
        wdwT = R5[:, 512:512 + KW * C]
        qT = RU[:, 0:C * T].rearrange("p (c t) -> p c t", c=C)
        oT = cv
        kT = RK[:, 0:C * NMEM].rearrange("p (c m) -> p c m", c=C)
        vM = RK[:, C * NMEM:2 * C * NMEM].rearrange("p (t d) -> p t d", t=2)
        hflat = hT[:, :, :].rearrange("p c t -> p (c t)")
        probs = hflat[:, 0:2048].rearrange("p (b s m) -> p b s m", b=4, s=2)
        pT = hflat[:, 2048:4096].rearrange("p (b m t) -> p b m t", b=2, m=2)
        walr = RU[:, C * T:C * T + C * RANK].rearrange("p (c r) -> p c r", c=C)
        wa2 = RC[0:RANK, 7 * T:8 * T]
        alr = RK[0:RANK, 7 * T:8 * T]
        vG = RC[:, :].rearrange("p (t d) -> p t d", t=TT)
        rG = RK[:, :].rearrange("p (c t) -> p c t", c=C)
        xg = hflat[:, 0:1024].rearrange("p (c s) -> p c s", c=C)
        yT = hflat[:, 1024:2048].rearrange("p (c s) -> p c s", c=C)
        sil = hflat[:, 2048:2560].rearrange("p (e f) -> p e f", e=2)
        hid = hflat[:, 2560:3072].rearrange("p (e f) -> p e f", e=2)

        PS = ctx.enter_context(nc.psum_tensor("PS", [P, 8 * BANK], F32))

        def bank(b, lo=0, hi=BANK):
            return PS[:, b * BANK + lo:b * BANK + hi]

        bank_full = [sem(f"bank_full{b}") for b in range(8)]
        bank_read = [sem(f"bank_read{b}") for b in range(8)]
        ring_ld = [sem(f"ring_ld{i}") for i in range(RING)]
        s_const = sem("s_const")
        s_constp = sem("s_constp")
        s_xld = sem("s_xld")
        s_mld = sem("s_mld")
        s_vld = sem("s_vld")
        s_gld = sem("s_gld")
        s_wr = sem("s_wr")
        sq_ready = sem("sq_ready")
        diag_ready = sem("diag_ready")
        h_ready = sem("h_ready")
        xm_ready = sem("xm_ready")
        silu_ready = sem("silu_ready")
        conv_step = sem("conv_step")
        act_chain = sem("act_chain")
        dve_chain = sem("dve_chain")
        mrms_ready = sem("mrms_ready")
        mem_ready = sem("mem_ready")
        nm_ready = sem("nm_ready")
        p_ready = sem("p_ready")
        ln_ready = sem("ln_ready")
        bc_ready = sem("bc_ready")
        gdiff_ready = sem("gdiff_ready")
        gexp_ready = sem("gexp_ready")
        gstage_done = sem("gstage_done")
        inter_done = sem("inter_done")
        osq_ready = sem("osq_ready")
        rin_ready = sem("rin_ready")
        rex_ready = sem("rex_ready")
        mask_ready = sem("mask_ready")
        hhi_ready = sem("hhi_ready")
        cnt_ready = sem("cnt_ready")
        moe_done = sem("moe_done")
        s_out = sem("s_out")
        SEG = ("onehot_ready", "gather_full", "xg_ready", "gu_full0", "gu_full1", "silu_done", "hid_ready",
               "y_full0", "y_full1", "yT_ready", "tr_full", "yhi_done", "y_split", "sc_full", "sc_read")
        seg = {(l, o): {x: sem(f"{x}_{l}{o}") for x in SEG} for l in range(DEPTH) for o in ("m", "o")}
        ov_ld = [[sem(f"ov_ld{l}_{i}") for i in range(RING)] for l in range(DEPTH)]

        ov_tables = [sem(f"ov_tables{l}") for l in range(DEPTH)]

        def full(key):
            b, k = plan.at[key]
            return bank_full[b], k + 1

        def read(key):
            b, k = plan.at[key]
            return bank_read[b], k + 1

        def vcol(name, i):
            return vecT[:, VROWS[name][0] + i:VROWS[name][0] + i + 1]

        norm_gain = [("norm_mix", 0), ("conv_ln_g", 0), ("norm_xattn", 0), ("norm_ffn", 0),
                     ("norm_mix", 8), ("norm_xattn", 8), ("norm_ffn", 8), ("norm_final", 0)]
        norm_key = [("xt",), None, ("co",), ("xo", 0), None, ("go",), ("xo", 1), None]
        norm_src = [cv if i == 1 else xT for i in range(8)]
        norm_dst = [cv if i == 1 else hT for i in range(8)]
        LAST = 7

        def norm_source(eng, i, c):
            if i == 2 and c == 0:
                eng.wait_ge(*full(("co", C - 1)))
            if norm_key[i] is not None:
                eng.wait_ge(*read(norm_key[i] + (c,)))
            elif i == 1:
                if c < C - 1:
                    eng.wait_ge(xm_ready, c + 1)
                else:
                    eng.wait_ge(*read(("mu_bc",)))
            elif c == 0:
                eng.wait_ge(moe_done, 1 if i == 4 else 2)

        def wait_h(eng, i, c):
            if c < C - 1:
                eng.wait_ge(h_ready, (C - 1) * i + c + 1)
            else:
                eng.wait_ge(*read(("rms_bc", i)))

        def slot_of(n):
            return ring[:, n % RING, :]

        block = ctx.enter_context(nc.Block())

        @block.tensor
        def _(pe):
            def take(key, b=None):
                b, k = plan.use(key, b)
                if k:
                    pe.wait_ge(bank_read[b], k)
                return b

            def tile(l, kind, i, key):
                n = tile_no[(l, kind, i)]
                pe.wait_ge(ring_ld[n % RING], 16 * (n // RING + 1))
                release[n] = key
                return slot_of(n)

            def group(o, lhs, rhs, nk):
                for k in range(nk):
                    mm = pe.matmul(o, lhs(k), rhs(k), start=(k == 0), stop=(k == nk - 1))
                return mm

            def token_sums(key, src, wait, b=None):
                b = take(key, b)
                n = len(src)
                for c in range(n):
                    wait(c)
                    for t in range(TT):
                        mm = pe.matmul(bank(b, t, t + 1), src[c][:, t * P:(t + 1) * P], ones[:, 0:1],
                                       start=(c == 0 and t == 0), stop=(c == n - 1), skip_group_check=True)
                mm.then_inc(bank_full[b], 1)

            diag = [0]

            def spread(key, b=None):
                b = take(key, b)
                for t in range(TT):
                    diag[0] += 1
                    pe.wait_ge(diag_ready, diag[0])
                    mm = pe.matmul(bank(b, t * P, (t + 1) * P), ones[:, :], dg[:, t, :], start=True, stop=True)
                mm.then_inc(bank_full[b], 1)

            def norm(i):
                token_sums(("rms", i), [hT[:, c, :] for c in range(C)],
                           lambda c: pe.wait_ge(sq_ready, C * i + c + 1))
                spread(("rms_bc", i))

            def project(l, kind, i, key, src, wait=None):
                w = tile(l, kind, i, key + (4 * i + 3,))
                for m in range(4):
                    project_chunk(w, m, key + (4 * i + m,), src, wait if m == 0 else None)

            def project_chunk(w, m, key, src, wait=None):
                b = take(key)
                for k in range(C):
                    if wait is not None:
                        wait(k)
                    mm = pe.matmul(bank(b), w[:, k * 512 + m * P:k * 512 + (m + 1) * P], src[:, k, :],
                                   start=(k == 0), stop=(k == C - 1))
                mm.then_inc(bank_full[b], 1)

            def transposes(key, pairs):
                b = take(key)
                for j, src in enumerate(pairs):
                    mm = pe.transpose(bank(b, j * P, (j + 1) * P), src, ident[:, :])
                mm.then_inc(bank_full[b], 1)

            def mem_kv(l):
                for i in range(2):
                    w = tile(l, "kv", i, ("k", l, 2 * i + 1))
                    for jj in range(2):
                        b = take(("k", l, 2 * i + jj))
                        for m in (2 * jj, 2 * jj + 1):
                            mm = group(bank(b, (m % 2) * NMEM, (m % 2 + 1) * NMEM),
                                       lambda k: w[:, k * 512 + m * P:k * 512 + (m + 1) * P],
                                       lambda k: memT[:, k, :], C)
                        mm.then_inc(bank_full[b], 1)
                for i in range(2):
                    w = tile(l, "kv", 2 + i, ("v", l, i, 1))
                    for mt in range(2):
                        b = take(("v", l, i, mt))
                        group(bank(b), lambda k: memT[:, k, mt * P:(mt + 1) * P],
                              lambda k: w[:, k * 512:(k + 1) * 512], C).then_inc(bank_full[b], 1)

            def attention(l):
                def scores(h):
                    for c in (2 * h, 2 * h + 1):
                        pe.wait_ge(*read(("q", l, c)))
                    for sp in range(2):
                        b = take(("s", l, h, sp))
                        for st in range(2):
                            t = 2 * sp + st
                            mm = group(bank(b, st * NMEM, (st + 1) * NMEM),
                                       lambda j: qT[:, 2 * h + j, t * P:(t + 1) * P],
                                       lambda j: kT[:, 2 * h + j, :], 2)
                        mm.then_inc(bank_full[b], 1)

                def values(h):
                    pe.wait_ge(p_ready, 8 * l + 2 * h + 2)
                    for mc in range(2):
                        transposes(("pt", l, h, mc),
                                   [probs[:, (2 * h + t // 2) % 4, t % 2, mc * P:(mc + 1) * P] for t in range(TT)])
                    for mc in range(2):
                        pe.wait_ge(*read(("pt", l, h, mc)))
                    for c in (2 * h, 2 * h + 1):
                        b = take(("o", l, c))
                        group(bank(b), lambda mc: vM[:, mc, c * P:(c + 1) * P],
                              lambda mc: pT[:, h % 2, mc, :], 2).then_inc(bank_full[b], 1)

                ni = 2 if l == 0 else 5
                norm(ni)
                for i in range(2):
                    project(l, "xq", i, ("q", l), hT, (lambda k: wait_h(pe, ni, k)) if i == 0 else None)
                for j in range(4):
                    pe.wait_ge(*read(("k", l, j)))
                    pe.wait_ge(*read(("v", l, j // 2, j % 2)))
                scores(0)
                for h in range(HEADS):
                    if h + 1 < HEADS:
                        scores(h + 1)
                    values(h)
                for i in range(2):
                    project(l, "xo", i, ("xo", l), oT,
                            (lambda k: pe.wait_ge(*read(("o", l, k)))) if i == 0 else None)

            def moe_segment(l, o, q0, nq):
                g = seg[(l, o)]
                base = moe_base[l] if o == "m" else 0
                ld = ring_ld if o == "m" else ov_ld[l]
                gate_up = (2, 3)
                ybank = 4
                scb = (6, 7)

                def wtile(i, j):
                    n = base + j
                    pe.wait_ge(ld[n % RING], 16 * (n // RING + 1) + 16 * i)
                    return slot_of(n)

                def gather(i):
                    pe.wait_ge(g["onehot_ready"], i + 1)
                    for c in range(C):
                        for t in range(TT):
                            for part in (hhi, hlo):
                                mm = pe.matmul(bank(0, c * P, (c + 1) * P), part[:, t, c * P:(c + 1) * P],
                                               onehot[:, t, :], start=(t == 0 and part is hhi),
                                               stop=(t == TT - 1 and part is hlo))
                        if c % 4 == 3:
                            mm.then_inc(g["gather_full"], 1)

                def up(i, e):
                    for b in range(2):
                        pe.wait_ge(g["xg_ready"], 2 * i + b + 1)
                    for half in range(2):
                        w = wtile(i, 2 * e + half)
                        for f in range(FC):
                            o0 = half * 256 + f * SL
                            mm = group(bank(gate_up[e], o0, o0 + SL),
                                       lambda k: w[:, k * FE + f * P:k * FE + (f + 1) * P],
                                       lambda k: xg[:, k, e * SL:(e + 1) * SL], C)
                    mm.then_inc(g[f"gu_full{e}"], 1)

                def down(i, e):
                    pe.wait_ge(g["hid_ready"], 2 * i + e + 1)
                    w = wtile(i, 4 + e)
                    for c in range(C):
                        o0 = c * P + e * SL
                        mm = group(bank(ybank, o0, o0 + SL),
                                   lambda f: w[:, f * D + c * P:f * D + (c + 1) * P],
                                   lambda f: hid[:, e, f * SL:(f + 1) * SL], FC)
                    mm.then_inc(g[f"y_full{e}"], 1)

                def back(i):
                    for c in range(C):
                        if c % 4 == 0:
                            pe.wait_ge(g["yT_ready"], 2 * i + c // 4 + 1)
                        mm = pe.transpose(bank(0, c * P, (c + 1) * P), yT[:, c, :], ident[:, :])
                        if c % 4 == 3:
                            mm.then_inc(g["tr_full"], 1)

                def scatter(i1):
                    for c in range(C):
                        if c % 4 == 0:
                            pe.wait_ge(g["y_split"], 2 * i1 - 1 + c // 4)
                        pe.wait_ge(g["sc_read"], 10 * i1 - 9 + c)
                        for part in (yhi, ylo):
                            mm = pe.matmul(bank(scb[c % 2]), part[:, c * P:(c + 1) * P], onehotT[:, :],
                                           start=(part is yhi), stop=(part is ylo))
                        mm.then_inc(g["sc_full"], 1)

                def slots(i, first):
                    if not first:
                        pe.wait_ge(g["sc_read"], 10 * i - 1)
                    for t in range(TT):
                        mm = pe.matmul(bank(scb[0], t * P, (t + 1) * P), onehot[:, t, :], identR[:, :],
                                       start=True, stop=True)
                    mm.then_inc(g["sc_full"], 1)
                    if not first:
                        pe.wait_ge(g["sc_read"], 10 * i)
                    group(bank(scb[1], 0, 2), lambda t: onehot[:, t, :].bitcast(F32),
                          lambda t: gpair[:, 2 * t:2 * t + 2], TT).then_inc(g["sc_full"], 1)

                def step(i, first, last):
                    up(i, 0)
                    if not first:
                        back(i - 1)
                    up(i, 1)
                    if not first:
                        scatter(i)
                    slots(i, first)
                    down(i, 0)
                    if not last:
                        gather(i + 1)
                    down(i, 1)

                gather(0)
                step(0, True, False)
                with pe.Fori(1, nq - 1) as i:
                    step(i, False, False)
                step(nq - 1, False, True)
                back(nq - 1)
                scatter(nq)

            pe.wait_ge(s_constp, 9)
            pe.wait_ge(s_vld, 16 * 14)
            b = take(("vt",))
            pe.transpose(bank(b, 0, NVEC), vrows[0:NVEC, 0:P], ident[0:NVEC, 0:NVEC])
            for j in (1, 2):
                mm = pe.transpose(bank(b, j * P, j * P + WDW_ROWS), vrows[0:WDW_ROWS, j * P:(j + 1) * P],
                                  ident[0:WDW_ROWS, 0:WDW_ROWS])
            mm.then_inc(bank_full[b], 1)
            pe.wait_ge(s_xld, 16)
            for c in range(C):
                transposes(("xt", c), [x_tm[:, t, c * P:(c + 1) * P] for t in range(TT)])
            norm(0)
            for half in range(2):
                wa = tile(0, "conv_in", half, ("a", 4 * half + 3))
                wg = tile(0, "conv_in", 2 + half, ("g", 4 * half + 3))
                for m in range(4):
                    c = 4 * half + m
                    project_chunk(wa, m, ("a", c), hT, (lambda k: wait_h(pe, 0, k)) if c == 0 else None)
                    project_chunk(wg, m, ("g", c), hT)
            pe.wait_ge(mem_ready, 2)
            for j in range(4):
                transposes(("mt", j), [mem_tm[:, mt, c * P:(c + 1) * P] for c in (2 * j, 2 * j + 1) for mt in range(2)])
            for j in range(4):
                pe.wait_ge(*read(("mt", j)))
            mem_kv(0)
            token_sums(("mu",), [cv[:, c, :] for c in range(C)],
                       lambda c: pe.wait_ge(conv_step, 2 * KW * (c // 2 + 1)))
            spread(("mu_bc",))
            norm(1)
            for i in range(2):
                project(0, "conv_out", i, ("co",), hT, (lambda k: pe.wait_ge(silu_ready, k + 1)) if i == 0 else None)
            attention(0)

            def moe(l):
                ni = 3 + 3 * l
                norm(ni)
                b = take(("lg", l))
                pe.wait_ge(s_wr, 64 * (l + 1))
                for c in range(C):
                    wait_h(pe, ni, c)
                for t in range(TT):
                    o = bank(b, t * (NG + NE), (t + 1) * (NG + NE))
                    for k in range(C):
                        pe.matmul(o, hT[:, k, t * P:(t + 1) * P], wr[:, k, :], start=(k == 0), stop=False)
                    mm = pe.matmul(o, ones[0:1, :], brow[0:1, :], start=False, stop=True)
                mm.then_inc(bank_full[b], 1)
                for t in range(TT):
                    for half in range(2):
                        transposes(("ht", l, t, half),
                                   [hT[:, 4 * half + j, t * P:(t + 1) * P] for j in range(4)])
                b = take(("cs", l))
                pe.wait_ge(mask_ready, l + 1)
                mk = rt[:, 0:TT * NE].rearrange("p (t e) -> p t e", t=TT)
                for t in range(TT):
                    for s in range(t + 1):
                        pe.matmul(bank(b, t * NE, (t + 1) * NE), (tri if s == t else ones)[:, :], mk[:, s, :],
                                  start=(s == 0), stop=(s == t))
                group(bank(b, TT * NE, (TT + 1) * NE), lambda s: ones[:, :], lambda s: mk[:, s, :],
                      TT).then_inc(bank_full[b], 1)
                for b in range(8):
                    pe.wait_ge(bank_read[b], plan.uses[b])
                moe_segment(l, "m", 0, PAIRS)
                pe.wait_ge(cnt_ready, l + 1)
                worst = pe.value_load(cnt_i[0:1, l:l + 1], min_val=0, max_val=T)
                with pe.If(worst > SL):
                    pe.wait_ge(seg[(l, "m")]["sc_read"], 10 * PAIRS)
                    moe_segment(l, "o", PAIRS, (ROUNDS - 1) * PAIRS)

            moe(0)
            norm(4)
            project(1, "gla_in", 0, ("gq",), hT, lambda k: wait_h(pe, 4, k))
            project(1, "gla_in", 1, ("gq",), hT)
            pe.wait_ge(s_gld, 32)
            b = take(("alr",))
            group(PS[0:RANK, b * BANK:(b + 1) * BANK], lambda k: walr[:, k, :], lambda k: hT[:, k, :],
                  C).then_inc(bank_full[b], 1)
            pe.wait_ge(*read(("alr",)))
            for h in range(HEADS):
                b = take(("z", h))
                pe.matmul(bank(b), wa2[:, h * DK:(h + 1) * DK], alr, start=True, stop=True).then_inc(bank_full[b], 1)
            for half in range(2):
                w = tile(1, "gla_v", half, ("gv", half, TT - 1))
                for t in range(TT):
                    b = take(("gv", half, t))
                    group(bank(b), lambda k: hT[:, k, t * P:(t + 1) * P],
                          lambda k: w[:, k * 512:(k + 1) * 512], C).then_inc(bank_full[b], 1)
            for i in range(2):
                project(1, "gla_r", i, ("gr",), hT)
            for b in range(8):
                pe.wait_ge(bank_read[b], plan.uses[b])

            def gla_norm(h):
                token_sums(("gs", h), [EB[:, j, :] for j in range(2)],
                           lambda j: pe.wait_ge(osq_ready, 2 * h + j + 1), b=2)
                spread(("gb", h), b=3)

            for h in range(HEADS):
                pe.wait_ge(gstage_done, h + 1)
                b = take(("att", h), 2)
                for t in range(TT):
                    mm = pe.matmul(bank(b, t * P, (t + 1) * P), qT[:, 4 + h, t * P:(t + 1) * P],
                                   qT[:, h, t * P:(t + 1) * P], start=True, stop=True)
                mm.then_inc(bank_full[b], 1)
                b = take(("kd", h), 3)
                for t in range(TT):
                    mm = pe.transpose(bank(b, t * P, (t + 1) * P), hT[:, 4 + h, t * P:(t + 1) * P], ident[:, :])
                mm.then_inc(bank_full[b], 1)
                ob = (0, 1) if h % 2 == 0 else (6, 7)

                def update(c):
                    b = take(("u", h, c), 4 + c % 2)
                    lo, t = CH * (c % 2), c // 2
                    pe.matmul(bank(b, 0, 256), R5[lo:lo + CH, h * T + t * P:h * T + (t + 1) * P],
                              vG[lo:lo + CH, t, h * 256:(h + 1) * 256], start=True,
                              stop=True).then_inc(bank_full[b], 1)

                pe.wait_ge(*read(("kd", h)))
                update(0)
                update(1)
                if h:
                    gla_norm(h - 1)
                pe.wait_ge(*read(("att", h)))
                for j in range(2):
                    take(("go_ps", h, j), ob[j])
                for t in range(TT):
                    for j in range(2):
                        pe.matmul(bank(ob[j], t * P, (t + 1) * P), vG[:, t, h * 256 + j * P:h * 256 + (j + 1) * P],
                                  AT[:, t, :], start=True, stop=False, skip_group_check=True)
                    for c in (2 * t, 2 * t + 1):
                        if c == 0:
                            continue
                        pe.wait_ge(*read(("u", h, c - 1)))
                        for j in range(2):
                            mm = pe.matmul(bank(ob[j], c * CH, (c + 1) * CH), SS[:, c % 2, j * P:(j + 1) * P],
                                           hT[:, h, c * CH:(c + 1) * CH], start=False, stop=True,
                                           skip_group_check=True)
                            if c == NCH - 1:
                                mm.then_inc(bank_full[ob[j]], 1)
                        if c <= NCH - 3:
                            mm.then_inc(inter_done, 1)
                    for c in (2 * t + 2, 2 * t + 3):
                        if c < NCH - 1:
                            update(c)
            gla_norm(HEADS - 1)
            for i in range(2):
                project(1, "gla_o", i, ("go",), rG,
                        (lambda k: pe.wait_ge(*read(("go_ps", k // 2, k % 2)))) if i == 0 else None)
            mem_kv(1)
            attention(1)
            moe(1)
            norm(LAST)
            for c in range(C):
                wait_h(pe, LAST, c)
            for t in range(TT):
                for half in range(2):
                    transposes(("out", t, half), [hT[:, 4 * half + j, t * P:(t + 1) * P] for j in range(4)])

        @block.sync
        def _(sp):
            def dram(l, kind, i):
                cols = slice(i * 512, (i + 1) * 512)
                if kind == "conv_in":
                    w = a["conv_w_in"][0][:, cols]
                elif kind == "conv_out":
                    w = a["conv_w_out"][0][:, cols]
                elif kind == "kv":
                    w = a["xa_w_kv"][l][:, cols]
                elif kind == "xq":
                    w = a["xa_w_q"][l][:, cols]
                elif kind == "xo":
                    w = a["xa_w_o"][l][:, cols]
                elif kind == "gla_o":
                    w = a["gla_w_o"][0][:, cols]
                else:
                    first = {"gla_in": 0, "gla_v": 1024, "gla_r": 2048 + RANK}[kind] + i * 512
                    w = a["gla_w_in"][0][:, first:first + 512]
                return w.rearrange("(k p) n -> p k n", p=P)

            def dst(n, nk):
                return slot_of(n).rearrange("p (k n) -> p k n", k=nk)

            def expert(l, pair, j):
                if j < 4:
                    w = a["moe_w_gate" if j % 2 == 0 else "moe_w_up"][l, 2 * pair + j // 2]
                else:
                    w = a["moe_w_down"][l, 2 * pair + j - 4]
                return w.rearrange("(k p) n -> p k n", p=P), (C if j < 4 else FC)

            def pair_release(g, j, value):
                name = ("gu_full0", "gu_full0", "gu_full1", "gu_full1", "y_full0", "y_full1")[j]
                sp.wait_ge(g[name], value)

            for l in range(DEPTH):
                main, over = seg[(l, "m")], seg[(l, "o")]
                for t in tiles[l]:
                    n = tile_no[(l,) + t]
                    if n - RING in release:
                        sp.wait_ge(*full(release[n - RING]))
                    elif n >= RING:
                        pair_release(seg[(l - 1, "m")], (n - RING - moe_base[l - 1]) % RING, PAIRS)
                    sp.dma_start(dst(n, C), dram(l, *t)).then_inc(ring_ld[n % RING], 16)
                base = moe_base[l]
                for j in range(6):
                    n = base + j
                    sp.wait_ge(*full(release[n - RING]))
                    src, nk = expert(l, 0, j)
                    sp.dma_start(dst(n, nk), src).then_inc(ring_ld[n % RING], 16)
                with sp.Fori(1, PAIRS) as i:
                    for j in range(6):
                        n = base + j
                        pair_release(main, j, i)
                        src, nk = expert(l, i, j)
                        sp.dma_start(dst(n, nk), src).then_inc(ring_ld[n % RING], 16)
                sp.wait_ge(cnt_ready, l + 1)
                worst = sp.value_load(cnt_i[0:1, l:l + 1], min_val=0, max_val=T)
                with sp.If(worst > SL):
                    def over_tiles(pair, done):
                        for j in range(6):
                            if done is not None:
                                pair_release(over, j, done)
                            src, nk = expert(l, pair, j)
                            sp.dma_start(dst(j, nk), src).then_inc(ov_ld[l][j], 16)
                    for j in range(6):
                        pair_release(main, j, PAIRS)
                    over_tiles(0, None)
                    with sp.Fori(1, PAIRS) as i:
                        over_tiles(i, i)
                    with sp.Fori(1, ROUNDS - 1) as r:
                        with sp.Fori(0, PAIRS) as i:
                            over_tiles(i, PAIRS * r + i)
                    for j in range(6):
                        pair_release(over, j, (ROUNDS - 1) * PAIRS)
            o_dram = out.rearrange("b (t p) d -> (b t) p d", p=P)
            for t in range(TT):
                for half in range(2):
                    sp.wait_ge(*read(("out", t, half)))
                sp.dma_start(o_dram[t], x_tm[:, t, :]).then_inc(s_out, 16)
            sp.wait_ge(s_out, 16 * TT)

        @block.gpsimd
        def _(pool):
            n_dma = 0
            for name, (r0, rows) in VROWS.items():
                v = a[name]
                v = v.rearrange("(c p) -> c p", p=P) if len(v.shape) == 1 else v.rearrange("l (c p) -> (l c) p", p=P)
                pool.dma_start(vrows[r0:r0 + rows, 0:P], v).then_inc(s_vld, 16)
            w = a["conv_w_dw"][0].rearrange("k (c p) -> (k c) p", p=P)
            for j in range(2):
                pool.dma_start(vrows[0:WDW_ROWS, (j + 1) * P:(j + 2) * P],
                               w[j * WDW_ROWS:(j + 1) * WDW_ROWS, :]).then_inc(s_vld, 16)
            pool.memset(ident[:, :], 0.0).then_inc(s_constp, 1)
            pool.memset(ones[:, :], 1.0).then_inc(s_constp, 1)
            pool.memset(tri[:, :], 1.0).then_inc(s_constp, 1)
            pool.memset(gmask[:, :], 1.0).then_inc(s_constp, 1)
            pool.wait_ge(s_constp, 4)
            pool.affine_select(out=ident[:, :], in_=ident[:, :], compare_op=ALU.not_equal, fill=1.0, base=0,
                               pattern=[[-1, P]], channel_multiplier=1).then_inc(s_constp, 1)
            pool.affine_select(out=tri[:, :], in_=tri[:, :], compare_op=ALU.is_gt, fill=0.0, base=0,
                               pattern=[[1, P]], channel_multiplier=-1).then_inc(s_constp, 1)
            pool.affine_select(out=gmask[:, :], in_=gmask[:, :], compare_op=ALU.is_ge, fill=0.0, base=0,
                               pattern=[[1, P]], channel_multiplier=-1).then_inc(s_constp, 1)
            pool.wait_ge(s_constp, 7)
            pool.memset(gmask[0:CH, CH:P], 0.0).then_inc(s_constp, 1)
            pool.iota(iota[:, :], pattern=[[1, SL]], base=0, channel_multiplier=0,
                      allow_small_or_imprecise_dtypes=True).then_inc(s_constp, 1)
            for l in range(DEPTH):
                if l == 1:
                    pool.wait_ge(moe_done, 1)
                    with nc.allow_non_contiguous_dma(reason="16 columns of a wide matrix"):
                        pool.dma_start(walr, a["gla_w_in"][0][:, 2048:2048 + RANK].rearrange("(k p) n -> p k n", p=P)
                                       ).then_inc(s_gld, 16)
                    pool.dma_start(wa2, a["gla_w_a2"][0]).then_inc(s_gld, 16)
                for c in range(C):
                    pool.wait_ge(*read(("xo", l, c)))
                ws = [(wr[:, :, 0:NG], a["moe_w_grp"][l].rearrange("(k p) n -> p k n", p=P)),
                      (wr[:, :, NG:], a["moe_w_exp"][l].rearrange("(k p) n -> p k n", p=P)),
                      (brow[:, 0:NG], a["moe_b_grp"][l:l + 1, :]), (brow[:, NG:], a["moe_b_exp"][l:l + 1, :])]
                for d, s in ws:
                    pool.dma_start(d, s).then_inc(s_wr, 16)

        @block.scalar
        def _(act):
            chain = [0]

            def link(ins):
                chain[0] += 1
                ins.then_inc(act_chain, 1)
                act.wait_ge(act_chain, chain[0])

            def evacuate(key, dst, scale=1.0, lo=0, hi=BANK):
                act.wait_ge(*full(key))
                b = plan.at[key][0]
                act.activation(dst, bank(b, lo, hi), ACT.Copy, scale=scale).then_inc(bank_read[b], 1)

            def norm(i):
                for c in range(C):
                    norm_source(act, i, c)
                    act.activation(hT[:, c, :], norm_src[i][:, c, :], ACT.Square).then_inc(sq_ready, 1)
                act.wait_ge(*full(("rms", i)))
                b = plan.at[("rms", i)][0]
                act.activation(rstat, bank(b, 0, TT), ACT.Sqrt, bias=EPS, scale=1.0 / D).then_inc(bank_read[b], 1)

            def mem_kv(l):
                for j in range(4):
                    evacuate(("k", l, j), RK[:, j * 512:(j + 1) * 512])
                for i in range(2):
                    for mt in range(2):
                        evacuate(("v", l, i, mt), vM[:, mt, i * 512:(i + 1) * 512])

            def attention(l):
                def softmax(h):
                    if h >= 2:
                        act.wait_ge(*full(("pt", l, h - 2, 1)))
                    for sp in range(2):
                        unit = 2 * h + sp
                        act.wait_ge(nm_ready, 8 * l + unit + 1)
                        b = plan.at[("s", l, h, sp)][0]
                        for st in range(2):
                            col = 2 * unit + st
                            ins = act.activation(probs[:, unit % 4, st, :], bank(b, st * NMEM, (st + 1) * NMEM), ACT.Exp,
                                                 bias=nmaxs[:, col:col + 1], scale=1.0 / 16.0,
                                                 accum_out=ssum[:, col:col + 1])
                        ins.then_inc(bank_read[b], 1)

                norm(2 if l == 0 else 5)
                for c in range(C):
                    evacuate(("q", l, c), qT[:, c, :])
                for c in (7,):
                    act.wait_ge(*full(("q", l, c)))
                softmax(0)
                for h in range(HEADS):
                    if h + 1 < HEADS:
                        softmax(h + 1)
                    if h >= 2:
                        act.wait_ge(*full(("o", l, 2 * (h - 2) + 1)))
                    for mc in range(2):
                        evacuate(("pt", l, h, mc), pT[:, h % 2, mc, :])

            def moe_segment(l, o, nq):
                g = seg[(l, o)]

                def take_x(i):
                    for b in range(2):
                        act.wait_ge(g["gather_full"], 2 * i + b + 1)
                        act.activation(hflat[:, b * 512:(b + 1) * 512], bank(b), ACT.Copy).then_inc(g["xg_ready"], 1)

                def step(i, last):
                    for e in range(2):
                        act.wait_ge(g[f"gu_full{e}"], i + 1)
                        act.activation(sil[:, e, :], bank(2 + e, 0, 256), ACT.Silu).then_inc(g["silu_done"], 1)
                    if not last:
                        take_x(i + 1)
                    act.wait_ge(g["y_full1"], i + 1)
                    for b in range(2):
                        act.activation(hflat[:, 1024 + b * 512:1024 + (b + 1) * 512], bank(4 + b),
                                       ACT.Copy).then_inc(g["yT_ready"], 1)

                take_x(0)
                step(0, False)
                with act.Fori(1, nq - 1) as i:
                    step(i, False)
                step(nq - 1, True)

            def moe(l):
                norm(3 + 3 * l)
                for t in range(TT):
                    for half in range(2):
                        act.wait_ge(*full(("ht", l, t, half)))
                        b = plan.at[("ht", l, t, half)][0]
                        act.activation(hhi[:, t, half * 512:(half + 1) * 512], bank(b), ACT.Copy).then_inc(hhi_ready, 1)
                    if t == 0:
                        act.wait_ge(rin_ready, 2 * l + 1)
                        act.activation(rt[:, 576:592], rt[:, 560:576], ACT.Exp).then_inc(rex_ready, 1)
                    if t == 1:
                        act.wait_ge(rin_ready, 2 * l + 2)
                        act.activation(rt[:, 604:608], rt[:, 600:604], ACT.Exp).then_inc(rex_ready, 1)
                moe_segment(l, "m", PAIRS)
                act.wait_ge(cnt_ready, l + 1)
                worst = act.value_load(cnt_i[0:1, l:l + 1], min_val=0, max_val=T)
                with act.If(worst > SL):
                    moe_segment(l, "o", (ROUNDS - 1) * PAIRS)

            act.dma_start(x_tm[:, :, :], a["x"].rearrange("b (t p) d -> p (b t) d", p=P)).then_inc(s_xld, 16)
            act.dma_start(mem_tm[:, :, :], a["mem"].rearrange("b (t p) d -> p (b t) d", p=P)).then_inc(s_mld, 16)
            for c in range(1, C, 2):
                evacuate(("xt", c), xT[:, c, :])
            norm(0)
            act.wait_ge(s_mld, 16)
            ebf = EB[:, :, :].rearrange("p a t -> p (a t)")
            for mt in range(2):
                link(act.activation(ebf, mem_tm[:, mt, :], ACT.Square, accum_out=mstat[:, mt:mt + 1]))
            act.activation(mstat, mstat, ACT.Sqrt, bias=EPS, scale=1.0 / D).then_inc(mrms_ready, 1)
            for c in range(C):
                act.wait_ge(*full(("g", c)))
                if c >= 2:
                    act.wait_ge(*read(("a", c - 2)))
                b = plan.at[("g", c)][0]
                act.activation(EB[:, c % 2, :], bank(b), ACT.Sigmoid,
                               bias=vcol("conv_b_in", 8 + c)).then_inc(bank_read[b], 1)
            mem_kv(0)
            norm(1)
            for c in range(C):
                wait_h(act, 1, c)
                act.activation(hT[:, c, :], cv[:, c, :], ACT.Silu, bias=vcol("conv_ln_b", c)).then_inc(silu_ready, 1)
            attention(0)
            moe(0)
            norm(4)
            for c in range(C):
                evacuate(("gq", c), qT[:, c, :], scale=float(DK) ** -0.5 if c < HEADS else 1.0)
            b = plan.at[("alr",)][0]
            act.wait_ge(*full(("alr",)))
            act.activation(alr, PS[0:RANK, b * BANK:(b + 1) * BANK], ACT.Copy).then_inc(bank_read[b], 1)
            for h in range(HEADS):
                act.wait_ge(*full(("z", h)))
                if h >= 2:
                    act.wait_ge(bc_ready, h - 1)
                e = EB[:, h % 2, :]
                link(act.activation(e, bank(plan.at[("z", h)][0]), ACT.Abs, bias=vcol("gla_b_a", h)))
                link(act.activation(e, e, ACT.Exp, scale=-1.0))
                act.activation(e, e, ACT.Ln, bias=1.0).then_inc(ln_ready, 1)
            for h in range(HEADS):
                act.wait_ge(gdiff_ready, 2 * h + 2)
                atf = AT[:, :, :].rearrange("p a t -> p (a t)")
                ssf = SS[:, :, :].rearrange("p a t -> p (a t)")
                r5 = R5[:, h * T:(h + 1) * T]
                act.activation(atf, EB[:, 0, :], ACT.Exp, scale=1.0 / TAU).then_inc(gexp_ready, 1)
                act.activation(ssf, EB[:, 0, :], ACT.Exp, scale=-1.0 / TAU).then_inc(gexp_ready, 1)
                act.activation(r5, r5, ACT.Exp, scale=1.0 / TAU).then_inc(gexp_ready, 1)
                act.activation(EB[:, 1, :], EB[:, 1, :], ACT.Exp, scale=1.0 / TAU).then_inc(gexp_ready, 1)
            for c in range(C):
                act.wait_ge(*full(("gr", c)))
                b = plan.at[("gr", c)][0]
                act.activation(rG[:, c, :], bank(b), ACT.Silu).then_inc(bank_read[b], 1)

            def gla_norm(h):
                for j in range(2):
                    act.wait_ge(*full(("go_ps", h, j)))
                    if h == 0:
                        act.wait_ge(gstage_done, HEADS)
                    act.activation(EB[:, j, :], bank(plan.at[("go_ps", h, j)][0]), ACT.Square).then_inc(osq_ready, 1)
                act.wait_ge(*full(("gs", h)))
                b = plan.at[("gs", h)][0]
                act.activation(rstat, bank(b, 0, TT), ACT.Sqrt, bias=EPS, scale=1.0 / 256.0).then_inc(bank_read[b], 1)

            for h in range(HEADS):
                evacuate(("kd", h), R5[:, h * T:(h + 1) * T])
                if h:
                    gla_norm(h - 1)
            gla_norm(HEADS - 1)
            mem_kv(1)
            attention(1)
            moe(1)
            norm(LAST)
            for t in range(TT):
                evacuate(("out", t, 1), x_tm[:, t, 512:1024])

        @block.vector
        def _(dve):
            chain = [0]

            def link(ins):
                chain[0] += 1
                ins.then_inc(dve_chain, 1)
                dve.wait_ge(dve_chain, chain[0])

            def evacuate(key, dst):
                dve.wait_ge(*full(key))
                b = plan.at[key][0]
                dve.tensor_copy(dst, bank(b)).then_inc(bank_read[b], 1)

            def diagonals(vals):
                for t in range(TT):
                    dve.tensor_scalar(dg[:, t, :], ident[:, :], vals[:, t:t + 1], None, ALU.mult).then_inc(diag_ready, 1)

            def norm(i):
                dve.wait_ge(*read(("rms", i)))
                link(dve.reciprocal(rrec, rstat))
                diagonals(rrec)
                dve.wait_ge(*full(("rms_bc", i)))
                b = plan.at[("rms_bc", i)][0]
                name, g0 = norm_gain[i]
                for c in range(C):
                    dve.scalar_tensor_tensor(norm_dst[i][:, c, :], norm_src[i][:, c, :], vcol(name, g0 + c), bank(b),
                                             ALU.mult, ALU.mult).then_inc(h_ready if c < C - 1 else bank_read[b], 1)

            def residual(key, bias=None):
                for c in range(C):
                    dve.wait_ge(*full(key + (c,)))
                    b = plan.at[key + (c,)][0]
                    if bias is None:
                        ins = dve.tensor_tensor(xT[:, c, :], bank(b), xT[:, c, :], ALU.add)
                    else:
                        ins = dve.scalar_tensor_tensor(xT[:, c, :], bank(b), vcol(bias, c), xT[:, c, :],
                                                       ALU.add, ALU.add)
                    ins.then_inc(bank_read[b], 1)

            def attention(l):
                norm(2 if l == 0 else 5)

                def maxima(h):
                    for sp in range(2):
                        unit = 2 * h + sp
                        dve.wait_ge(*full(("s", l, h, sp)))
                        b = plan.at[("s", l, h, sp)][0]
                        cols = slice(2 * unit, 2 * unit + 2)
                        link(dve.tensor_reduce(nmax[:, cols], bank(b).rearrange("p (s m) -> p s m", s=2), AX.X, ALU.max))
                        dve.tensor_scalar(nmaxs[:, cols], nmax[:, cols], -1.0 / 16.0, None,
                                          ALU.mult).then_inc(nm_ready, 1)

                def normalise(h):
                    for sp in range(2):
                        unit = 2 * h + sp
                        dve.wait_ge(*read(("s", l, h, sp)))
                        cols = slice(2 * unit, 2 * unit + 2)
                        link(dve.reciprocal(srec[:, cols], ssum[:, cols]))
                        r = srec[:, cols].unsqueeze(2).to_broadcast([P, 2, NMEM])
                        dve.tensor_tensor(probs[:, unit % 4], probs[:, unit % 4], r, ALU.mult).then_inc(p_ready, 1)

                maxima(0)
                for h in range(HEADS):
                    normalise(h)
                    if h + 1 < HEADS:
                        maxima(h + 1)
                    for c in (2 * h, 2 * h + 1):
                        evacuate(("o", l, c), oT[:, c, :])
                residual(("xo", l))

            def router(l):
                W = NG + NE
                b = plan.at[("lg", l)][0]
                dve.wait_ge(*full(("lg", l)))
                dve.tensor_copy(lg[:, :, :], bank(b, 0, TT * W).rearrange("p (t w) -> p t w", t=TT)
                                ).then_inc(bank_read[b], 1)
                dve.wait_ge(*read(("lg", l)))
                gl = lg[:, :, 0:NG]
                el = lg[:, :, NG:W].rearrange("p t (g e) -> p t g e", g=NG)

                def v(o, n):
                    return rt[:, o:o + TT * n].rearrange("p (t n) -> p t n", t=TT)

                mask, mx, eq, idx = v(0, NE), v(128, 1), v(132, EG), v(164, 1)
                ohg, sel4, els = v(168, NG), v(184, NE), v(312, EG)
                oh1, oh2, m2, els2 = v(344, EG), v(376, EG), v(408, 1), v(412, EG)
                gv = v(444, EG)
                gin, gex, gsum, grec = v(560, NG), v(576, NG), v(592, 1), v(596, 1)
                din, dex, den = v(600, 1), v(604, 1), v(608, 1)

                def wide(x, n):
                    return x.to_broadcast([P, TT, n])

                def first_of(values, top, n, hot):
                    io = iota[:, 0:n].unsqueeze(1).to_broadcast([P, TT, n])
                    e = eq[:, :, 0:n]
                    link(dve.tensor_tensor(e, values, wide(top, n), ALU.is_equal))
                    link(dve.scalar_tensor_tensor(e, e, -float(EG), io, ALU.mult, ALU.add))
                    link(dve.tensor_reduce(idx, e, AX.X, ALU.min))
                    link(dve.tensor_scalar(idx, idx, float(EG), None, ALU.add))
                    link(dve.tensor_tensor(hot, io, wide(idx, n), ALU.is_equal))

                link(dve.tensor_reduce(mx, gl, AX.X, ALU.max))
                dve.tensor_tensor(gin, gl, wide(mx, NG), ALU.subtract).then_inc(rin_ready, 1)
                first_of(gl, mx, NG, ohg)
                for t in range(TT):
                    ins = dve.tensor_tensor(sel4[:, t, :].rearrange("p (g e) -> p g e", g=NG), el[:, t],
                                            ohg[:, t, :].unsqueeze(2).to_broadcast([P, NG, EG]), ALU.mult)
                    link(ins)
                for t in range(TT):
                    link(dve.tensor_reduce(els[:, t, :], sel4[:, t, :].rearrange("p (g e) -> p e g", g=NG),
                                           AX.X, ALU.add))
                link(dve.tensor_reduce(mx, els, AX.X, ALU.max))
                first_of(els, mx, EG, oh1)
                link(dve.scalar_tensor_tensor(els2, oh1, -BIG, els, ALU.mult, ALU.add))
                link(dve.tensor_reduce(m2, els2, AX.X, ALU.max))
                dve.tensor_tensor(din, m2, mx, ALU.subtract).then_inc(rin_ready, 1)
                first_of(els2, m2, EG, oh2)
                link(dve.tensor_tensor(els, oh1, oh2, ALU.add))
                for t in range(TT):
                    ins = dve.tensor_tensor(mask[:, t, :].rearrange("p (g e) -> p g e", g=NG),
                                            ohg[:, t, :].unsqueeze(2).to_broadcast([P, NG, EG]),
                                            els[:, t, :].unsqueeze(1).to_broadcast([P, NG, EG]), ALU.mult)
                    if t < TT - 1:
                        link(ins)
                    else:
                        ins.then_inc(mask_ready, 1)
                dve.wait_ge(rex_ready, 2 * l + 2)
                link(dve.tensor_reduce(gsum, gex, AX.X, ALU.add))
                link(dve.tensor_scalar(den, dex, 1.0, None, ALU.add))
                link(dve.tensor_tensor(gsum, gsum, den, ALU.mult))
                link(dve.reciprocal(grec, gsum))
                link(dve.tensor_tensor(gsum, grec, dex, ALU.mult))
                link(dve.tensor_tensor(oh1, oh1, wide(grec, EG), ALU.mult))
                link(dve.tensor_tensor(oh2, oh2, wide(gsum, EG), ALU.mult))
                link(dve.tensor_tensor(gv, oh1, oh2, ALU.add))
                for t in range(TT):
                    link(dve.tensor_tensor(sel4[:, t, :].rearrange("p (g e) -> p g e", g=NG),
                                           ohg[:, t, :].unsqueeze(2).to_broadcast([P, NG, EG]),
                                           gv[:, t, :].unsqueeze(1).to_broadcast([P, NG, EG]), ALU.mult))
                link(dve.tensor_copy(gtab[:, 0:PAIRS, :].rearrange("p q (t e) -> p q t e", e=2),
                                     sel4.rearrange("p t (q e) -> p q t e", e=2)))
                b = plan.at[("cs", l)][0]
                for t in range(TT):
                    for half in range(2):
                        k = (l * TT + t) * 2 + half
                        dve.wait_ge(hhi_ready, k + 1)
                        bt = plan.at[("ht", l, t, half)][0]
                        cols = slice(half * 512, (half + 1) * 512)
                        dve.tensor_tensor(hlo[:, t, cols], bank(bt), hhi[:, t, cols].bitcast(F32),
                                          ALU.subtract).then_inc(bank_read[bt], 1)
                dve.wait_ge(*full(("cs", l)))
                dve.wait_ge(mask_ready, l + 1)
                link(dve.scalar_tensor_tensor(sel4, bank(b, 0, TT * NE).rearrange("p (t e) -> p t e", t=TT), 1.0, mask,
                                              ALU.add, ALU.mult))
                link(dve.tensor_scalar(ptab[:, 0:PAIRS, :].rearrange("p q (t e) -> p q t e", e=2),
                                       sel4.rearrange("p t (q e) -> p q t e", e=2), -1.0, None, ALU.add))
                dve.tensor_reduce(maxc, bank(b, TT * NE, (TT + 1) * NE), AX.X, ALU.max).then_inc(bank_read[b], 1)
                dve.wait_ge(*read(("cs", l)))
                dve.tensor_copy(cnt_i[:, l:l + 1], maxc).then_inc(cnt_ready, 1)

            def moe_segment(l, o, q0, nq):
                g = seg[(l, o)]
                scb = (6, 7)

                def make_onehot(i):
                    dve.tensor_copy(gpair, gtab[:, i + q0, :])
                    r = ptab[:, i + q0, :].unsqueeze(2).to_broadcast([P, 2 * TT, SL])
                    dve.tensor_tensor(onehot[:, :, :].rearrange("p t (e s) -> p (t e) s", e=2),
                                      iota[:, :].unsqueeze(1).to_broadcast([P, 2 * TT, SL]), r,
                                      ALU.is_equal).then_inc(g["onehot_ready"], 1)

                def hidden(i, e):
                    dve.wait_ge(g["silu_done"], 2 * i + e + 1)
                    dve.tensor_tensor(hid[:, e, :], sil[:, e, :], bank(2 + e, 256, 512),
                                      ALU.mult).then_inc(g["hid_ready"], 1)

                def split_y(i1):
                    for b in range(2):
                        dve.wait_ge(g["tr_full"], 2 * i1 - 1 + b)
                        cols = slice(b * 512, (b + 1) * 512)
                        dve.tensor_scalar(yhi[:, cols], bank(b), gslot, None, ALU.mult).then_inc(g["yhi_done"], 1)
                        dve.wait_ge(g["yhi_done"], 2 * i1 - 1 + b)
                        dve.scalar_tensor_tensor(ylo[:, cols], bank(b), gslot, yhi[:, cols].bitcast(F32),
                                                 ALU.mult, ALU.subtract).then_inc(g["y_split"], 1)

                def accumulate(i1):
                    for c in range(C):
                        dve.wait_ge(g["sc_full"], 10 * i1 - 7 + c)
                        dve.tensor_tensor(xT[:, c, :], bank(scb[c % 2]), xT[:, c, :], ALU.add).then_inc(g["sc_read"], 1)

                def take_slots(i, first):
                    if not first:
                        dve.wait_ge(g["y_split"], 2 * i)
                    dve.wait_ge(g["sc_full"], 10 * i + 1)
                    dve.tensor_copy(onehotT[:, :], bank(scb[0])).then_inc(g["sc_read"], 1)
                    dve.wait_ge(g["sc_full"], 10 * i + 2)
                    dve.tensor_copy(gslot[0:SL, :], PS[0:SL, scb[1] * BANK:scb[1] * BANK + 1])
                    dve.tensor_copy(gslot[SL:P, :], PS[SL:P, scb[1] * BANK + 1:scb[1] * BANK + 2]
                                    ).then_inc(g["sc_read"], 1)
                    dve.wait_ge(g["sc_read"], 10 * i + 2)

                def step(i, first, last):
                    hidden(i, 0)
                    if not first:
                        split_y(i)
                    hidden(i, 1)
                    if not first:
                        accumulate(i)
                    take_slots(i, first)
                    if not last:
                        make_onehot(i + 1)

                make_onehot(0)
                step(0, True, False)
                with dve.Fori(1, nq - 1) as i:
                    step(i, False, False)
                step(nq - 1, False, True)
                split_y(nq)
                accumulate(nq)
                dve.wait_ge(g["sc_read"], 10 * nq)

            def moe(l):
                norm(3 + 3 * l)
                link(dve.tensor_copy(identR[:, :], ident[:, :]))
                router(l)
                moe_segment(l, "m", 0, PAIRS)
                dve.wait_ge(cnt_ready, l + 1)
                worst = dve.value_load(cnt_i[0:1, l:l + 1], min_val=0, max_val=T)
                with dve.If(worst > SL):
                    for r in range(1, ROUNDS):
                        q = slice(r * PAIRS, (r + 1) * PAIRS)
                        dve.tensor_scalar(ptab[:, q, :], ptab[:, 0:PAIRS, :], -float(r * SL), None,
                                          ALU.add).then_inc(ov_tables[l], 1)
                        dve.tensor_copy(gtab[:, q, :], gtab[:, 0:PAIRS, :]).then_inc(ov_tables[l], 1)
                    dve.wait_ge(ov_tables[l], 2 * (ROUNDS - 1))
                    moe_segment(l, "o", PAIRS, (ROUNDS - 1) * PAIRS)
                dve.memset(small[:, 130 + l:131 + l], 0.0).then_inc(moe_done, 1)

            dve.wait_ge(s_constp, 9)
            dve.memset(u[:, :, 0:KW - 1], 0.0).then_inc(s_const, 1)
            dve.wait_ge(*full(("vt",)))
            b = plan.at[("vt",)][0]
            dve.tensor_copy(vecT[:, :], bank(b, 0, NVEC))
            for j in range(2):
                ins = dve.tensor_copy(wdwT[:, j * WDW_ROWS:(j + 1) * WDW_ROWS],
                                      bank(b, (j + 1) * P, (j + 1) * P + WDW_ROWS))
            ins.then_inc(bank_read[b], 1)
            dve.wait_ge(*read(("vt",)))
            for c in range(0, C, 2):
                evacuate(("xt", c), xT[:, c, :])
            for c in range(C):
                dve.wait_ge(*read(("xt", c)))
            norm(0)
            dve.wait_ge(mrms_ready, 1)
            link(dve.reciprocal(mrec, mstat))
            for mt in range(2):
                dve.tensor_scalar(mem_tm[:, mt, :], mem_tm[:, mt, :], mrec[:, mt:mt + 1], None,
                                  ALU.mult).then_inc(mem_ready, 1)

            def glu(c):
                dve.wait_ge(*read(("g", c)))
                dve.wait_ge(*full(("a", c)))
                b = plan.at[("a", c)][0]
                dve.scalar_tensor_tensor(u[:, c, KW - 1:], bank(b), vcol("conv_b_in", c), EB[:, c % 2, :],
                                         ALU.add, ALU.mult).then_inc(bank_read[b], 1)

            def conv(c, k, step):
                if step >= 2:
                    dve.wait_ge(conv_step, step - 1)
                src = u[:, c, k:k + T]
                w = wdwT[:, k * C + c:k * C + c + 1]
                if k == 0:
                    ins = dve.tensor_scalar(cv[:, c, :], src, w, vcol("conv_b_dw", c), ALU.mult, ALU.add)
                else:
                    ins = dve.scalar_tensor_tensor(cv[:, c, :], src, w, cv[:, c, :], ALU.mult, ALU.add)
                ins.then_inc(conv_step, 1)

            dve.wait_ge(s_const, 1)
            step = 0
            for pair in range(C // 2):
                glu(2 * pair)
                glu(2 * pair + 1)
                for c in (2 * pair, 2 * pair + 1):
                    dve.wait_ge(*read(("a", c)))
                for k in range(KW):
                    for c in (2 * pair, 2 * pair + 1):
                        conv(c, k, step)
                        step += 1
                    if (pair, k) == (2, 20):
                      for j in range(4):
                        dve.wait_ge(*full(("mt", j)))
                        b = plan.at[("mt", j)][0]
                        for c in (2 * j, 2 * j + 1):
                            ins = dve.tensor_scalar(memT[:, c, :], bank(b, (c % 2) * NMEM, (c % 2 + 1) * NMEM),
                                                    vcol("norm_mem", c), None, ALU.mult)
                        ins.then_inc(bank_read[b], 1)
            dve.wait_ge(*full(("mu",)))
            b = plan.at[("mu",)][0]
            dve.tensor_scalar(musum, bank(b, 0, TT), 1.0 / D, None, ALU.mult).then_inc(bank_read[b], 1)
            dve.wait_ge(*read(("mu",)))
            diagonals(musum)
            dve.wait_ge(*full(("mu_bc",)))
            dve.wait_ge(conv_step, step)
            b = plan.at[("mu_bc",)][0]
            for c in range(C):
                dve.tensor_tensor(cv[:, c, :], cv[:, c, :], bank(b),
                                  ALU.subtract).then_inc(xm_ready if c < C - 1 else bank_read[b], 1)
            dve.wait_ge(*read(("mu_bc",)))
            norm(1)
            residual(("co",), "conv_b_out")
            for c in range(C):
                dve.wait_ge(*read(("co", c)))
            attention(0)
            for c in range(C):
                dve.wait_ge(*read(("xo", 0, c)))
            moe(0)
            norm(4)
            for h in range(HEADS):
                dve.wait_ge(ln_ready, h + 1)
                b = plan.at[("z", h)][0]
                r5 = R5[:, h * T:(h + 1) * T]
                dve.tensor_scalar(r5, bank(b), vcol("gla_b_a", h), 0.0, ALU.add, ALU.min).then_inc(bank_read[b], 1)
                dve.wait_ge(*read(("z", h)))
                link(dve.tensor_tensor(EB[:, h % 2, :], r5, EB[:, h % 2, :], ALU.subtract))
                for c in range(NCH):
                    sl = slice(c * CH, (c + 1) * CH)
                    ins = dve.tensor_tensor_scan(r5[:, sl], ones[:, 0:CH], EB[:, h % 2, sl], 0.0, ALU.mult, ALU.add)
                ins.then_inc(bc_ready, 1)
            for half in range(2):
                for t in range(TT):
                    evacuate(("gv", half, t), vG[:, t, half * 512:(half + 1) * 512])
            dve.wait_ge(bc_ready, HEADS)
            atf = AT[:, :, :].rearrange("p a t -> p (a t)")
            ssf = SS[:, :, :].rearrange("p a t -> p (a t)")
            for c in range(C):
                dve.wait_ge(*read(("gq", c)))
            dve.wait_ge(*full(("gr", C - 1)))
            for h in range(HEADS):
                r5 = R5[:, h * T:(h + 1) * T]
                bc = r5.rearrange("p (c j) -> p c j", c=NCH)
                if h:
                    dve.wait_ge(gstage_done, h)
                mid = bc[:, :, CH // 2 - 1:CH // 2].to_broadcast([P, NCH, CH])
                last = bc[:, :, CH - 1:CH].to_broadcast([P, NCH, CH])
                dve.tensor_tensor(EB[:, 0, :].rearrange("p (c j) -> p c j", c=NCH), bc, mid,
                                  ALU.subtract).then_inc(gdiff_ready, 1)
                dve.tensor_tensor(EB[:, 1, :].rearrange("p (c j) -> p c j", c=NCH), last, bc,
                                  ALU.subtract).then_inc(gdiff_ready, 1)
                dve.wait_ge(gexp_ready, 4 * h + 4)
                dve.tensor_copy(dec[:, h * NCH:(h + 1) * NCH], bc[:, :, CH - 1])
                dve.tensor_tensor(hT[:, h, :], qT[:, h, :], r5, ALU.mult)
                link(dve.tensor_tensor(hT[:, 4 + h, :], qT[:, 4 + h, :], EB[:, 1, :], ALU.mult))
                dve.tensor_tensor(qT[:, h, :], qT[:, h, :], atf, ALU.mult)
                dve.tensor_tensor(qT[:, 4 + h, :], qT[:, 4 + h, :], ssf, ALU.mult).then_inc(gstage_done, 1)
            dve.wait_ge(gstage_done, HEADS)
            link(dve.memset(AT[:, :, :], 0.0))

            def gla_norm(h):
                dve.wait_ge(*read(("gs", h)))
                link(dve.reciprocal(rrec, rstat))
                diagonals(rrec)
                dve.wait_ge(*full(("gb", h)))
                b = plan.at[("gb", h)][0]
                for j in range(2):
                    c = 2 * h + j
                    dve.wait_ge(*read(("gr", c)))
                    ins = dve.scalar_tensor_tensor(rG[:, c, :], rG[:, c, :], vcol("gla_norm_g", j), bank(b),
                                                   ALU.mult, ALU.mult)
                    if j == 0:
                        link(ins)
                    else:
                        ins.then_inc(bank_read[b], 1)
                dve.wait_ge(*read(("gb", h)))
                for j in range(2):
                    c = 2 * h + j
                    ob = plan.at[("go_ps", h, j)][0]
                    dve.tensor_tensor(rG[:, c, :], rG[:, c, :], bank(ob), ALU.mult).then_inc(bank_read[ob], 1)

            for h in range(HEADS):
                if h:
                    dve.wait_ge(*full(("go_ps", h - 1, 1)))
                dve.wait_ge(*full(("att", h)))
                b = plan.at[("att", h)][0]
                m = gmask[:, :].bitcast(U32).unsqueeze(1).to_broadcast([P, TT, P])
                dve.copy_predicated(AT[:, :, :], m, bank(b).rearrange("p (t i) -> p t i", t=TT)
                                    ).then_inc(bank_read[b], 1)
                if h:
                    gla_norm(h - 1)
                for c in range(1, NCH):
                    b = plan.at[("u", h, c - 1)][0]
                    kv = bank(b, 0, 256)
                    dve.wait_ge(*full(("u", h, c - 1)))
                    if c >= 3:
                        dve.wait_ge(inter_done, (NCH - 3) * h + c - 2)
                    if c == 1:
                        ins = dve.tensor_copy(SS[:, 1, :], kv)
                    else:
                        dve.wait_ge(*read(("u", h, c - 2)))
                        ins = dve.scalar_tensor_tensor(SS[:, c % 2, :], SS[:, (c - 1) % 2, :],
                                                       dec[:, h * NCH + c - 1:h * NCH + c], kv, ALU.mult, ALU.add)
                    ins.then_inc(bank_read[b], 1)
            gla_norm(HEADS - 1)
            residual(("go",))
            for c in range(C):
                dve.wait_ge(*read(("go", c)))
            attention(1)
            for c in range(C):
                dve.wait_ge(*read(("xo", 1, c)))
            moe(1)
            norm(LAST)
            for t in range(TT):
                evacuate(("out", t, 0), x_tm[:, t, 0:512])


_INS = ["x", "mem", "norm_mix", "norm_xattn", "norm_ffn", "norm_mem", "norm_final", "conv_w_in", "conv_b_in",
        "conv_w_dw", "conv_b_dw", "conv_ln_g", "conv_ln_b", "conv_w_out", "conv_b_out", "gla_w_in", "gla_w_a2",
        "gla_b_a", "gla_norm_g", "gla_w_o", "xa_w_q", "xa_w_kv", "xa_w_o", "moe_w_grp", "moe_b_grp", "moe_w_exp",
        "moe_b_exp", "moe_w_gate", "moe_w_up", "moe_w_down"]


def kernel(**inputs):
    import numpy as np
    import concourse.bacc as bacc
    from concourse.bass_utils import run_bass_kernel_spmd

    nc = bacc.Bacc("TRN2", target_bir_lowering=False, num_devices=1)
    arrays, args = {}, {}
    for name in _INS:
        arr = np.ascontiguousarray(inputs[name])
        arrays[f"in_{name}"] = arr
        args[name] = nc.dram_tensor(f"in_{name}", arr.shape, mybir.dt.from_np(arr.dtype), kind="ExternalInput").ap()
    out = nc.dram_tensor("out_0", (1, T, D), F32, kind="ExternalOutput").ap()
    build(nc, args, out)
    r = run_bass_kernel_spmd(nc, [arrays], core_ids=[0])
    return r.results[0]["out_0"]
```

```python
from contextlib import ExitStack

import concourse.bass as bass
from concourse import mybir

F32 = mybir.dt.float32
F32R = mybir.dt.float32r
I32 = mybir.dt.int32
U32 = mybir.dt.uint32
ALU = mybir.AluOpType
ACT = mybir.ActivationFunctionType
AX = mybir.AxisListType

P = 128
D = 1024
T = 512
DEPTH = 2
NMEM = 256
C = D // P
TT = T // P
EPS = 1e-6
KW = 31
PADW = T + KW - 1
HEADS = 4
DK = 128
CH = 64
NCH = T // CH
RANK = 16
TAU = 16.0
NG, EG = 4, 8
NE = NG * EG
FE = 512
FC = FE // P
SL = 64
ROUNDS = T // SL
QUAD = 4
NQ = NE // QUAD
PARTS = 4
PW = C * 512 // PARTS
WB = 4
RING = 4
POOL_UP = (3, 7)
POOL_DOWN = (2,)
AHEAD = 4
BANK = 512
BIG = 1.0e30

VROWS = {}
_n = 0
for _name, _rows in (("norm_mix", 16), ("norm_xattn", 16), ("norm_ffn", 16), ("norm_final", 8), ("norm_mem", 8),
                     ("conv_b_in", 16), ("conv_b_dw", 8), ("conv_ln_g", 8), ("conv_ln_b", 8), ("conv_b_out", 8),
                     ("gla_b_a", 4), ("gla_norm_g", 2)):
    VROWS[_name] = (_n, _rows)
    _n += _rows
NVEC = _n
NCONST = 13
WDW_ROWS = KW * C // 2


class BankPlan:

    def __init__(self):
        self.uses = [0] * 8
        self.next = 0
        self.at = {}

    def use(self, key, bank=None):
        if bank is None:
            bank = self.next
            self.next = (self.next + 1) % 8
        self.at[key] = (bank, self.uses[bank])
        self.uses[bank] += 1
        return self.at[key]


def weight_tiles():
    conv = [("conv_in", 0), ("conv_in", 2), ("conv_in", 1), ("conv_in", 3)]
    kv = [("kv", i) for i in range(4)]
    tail = [("xq", 0), ("xq", 1), ("xo", 0), ("xo", 1)]
    layer0 = conv + kv + [("conv_out", 0), ("conv_out", 1)] + tail
    layer1 = [("gla_in", 0), ("gla_in", 1), ("gla_v", 0), ("gla_v", 1), ("gla_r", 0), ("gla_r", 1),
              ("gla_o", 0), ("gla_o", 1)] + kv + tail
    return [layer0, layer1]


def build(nc, a, out):
    plan = BankPlan()
    tiles = weight_tiles()
    tile_no = {}
    n = 0
    moe_base = []
    for l in range(DEPTH):
        for t in tiles[l]:
            tile_no[(l,) + t] = n
            n += 1
        moe_base.append(n)
        n += 3 * NE
    release = {}

    with ExitStack() as ctx:
        def sb(name, shape, dt=F32, where=ctx):
            return where.enter_context(nc.sbuf_tensor(name, shape, dt))

        def sem(name):
            return ctx.enter_context(nc.semaphore(name))

        ring = sb("ring", [P, RING, C * 512])
        xT = sb("xT", [P, C, T])
        hT = sb("hT", [P, C, T])
        whi = sb("whi", [P, WB, PW], F32R)
        wlo = sb("wlo", [P, WB, PW], F32R)
        fold = sb("fold", [P, P])
        ident = sb("ident", [P, P])
        ones = sb("ones", [P, P])
        tri = sb("tri", [P, P])
        gmask = sb("gmask", [P, P])
        vecT = sb("vecT", [P, NVEC])
        memT = sb("memT", [P, C, NMEM])
        iota = sb("iota", [P, SL])
        small = sb("small", [P, 160])
        dg = sb("dg", [P, TT, P])
        cnt_i = sb("cnt_i", [P, DEPTH], I32)
        rstat = small[:, 0:4]
        rrec = small[:, 4:8]
        rms = dg[:, :, :].rearrange("p t s -> p (t s)")
        mstat = small[:, 8:10]
        mrec = small[:, 10:12]
        nmax = small[:, 12:28]
        nmaxs = small[:, 28:44]
        ssum = small[:, 44:60]
        srec = small[:, 60:76]
        dec = small[:, 76:108]
        maxc = small[:, 118:119]

        with ExitStack() as s:
            RU = sb("RU", [P, C * PADW], where=s)
            RC = sb("RC", [P, C * T], where=s)
            RK = sb("RK", [P, C * T], where=s)
            R5 = sb("R5", [P, HEADS * T], where=s)
            SS = sb("SS", [P, 2, 256], where=s)
            EB = sb("EB", [P, 2, T], where=s)
            AT = sb("AT", [P, TT, P], where=s)
        with ExitStack() as s:
            hhi = sb("hhi", [P, TT, D], F32R, where=s)
            hlo = sb("hlo", [P, TT, D], F32R, where=s)
            yhi = sb("yhi", [P, D], F32R, where=s)
            ylo = sb("ylo", [P, D], F32R, where=s)
            onehot = sb("onehot", [P, TT, QUAD * SL], F32R, where=s)
            onehotT = sb("onehotT", [P, T], F32R, where=s)
            identR = sb("identR", [P, P], F32R, where=s)
            with ExitStack() as before:
                wr = sb("wr", [P, C, NG + NE], where=before)
                brow = sb("brow", [1, NG + NE], where=before)
                lg = sb("lg", [P, TT, NG + NE], where=before)
                rt = sb("rt", [P, 640], where=before)
            xg = sb("xg", [P, C, QUAD, 2 * SL], F32R, where=s)
            hid = sb("hid", [P, FC, 2 * SL], F32R, where=s)
            ptab = sb("ptab", [P, NQ, TT * QUAD], where=s)
            gtab = sb("gtab", [P, NQ, TT * QUAD], where=s)
        u = RU[:, :].rearrange("p (c w) -> p c w", c=C)
        x_tm = RC[:, :].rearrange("p (t d) -> p t d", t=TT)
        cv = RC[:, :].rearrange("p (c t) -> p c t", c=C)
        mem_tm = RK[:, 0:2 * D].rearrange("p (t d) -> p t d", t=2)
        vrows = R5[:, 0:3 * P]
        wdwT = R5[:, 512:512 + KW * C]
        qT = RU[:, 0:C * T].rearrange("p (c t) -> p c t", c=C)
        oT = cv
        kT = RK[:, 0:C * NMEM].rearrange("p (c m) -> p c m", c=C)
        vM = RK[:, C * NMEM:2 * C * NMEM].rearrange("p (t d) -> p t d", t=2)
        hflat = hT[:, :, :].rearrange("p c t -> p (c t)")
        probs = hflat[:, 0:2048].rearrange("p (b s m) -> p b s m", b=4, s=2)
        pT = hflat[:, 2048:4096].rearrange("p (b m t) -> p b m t", b=2, m=2)
        walr = RU[:, C * T:C * T + C * RANK].rearrange("p (c r) -> p c r", c=C)
        wa2 = RC[0:RANK, 7 * T:8 * T]
        alr = RK[0:RANK, 7 * T:8 * T]
        vG = RC[:, :].rearrange("p (t d) -> p t d", t=TT)
        rG = RK[:, :].rearrange("p (c t) -> p c t", c=C)
        graw = hflat[:, 0:512]
        uraw = hflat[:, 512:1024]
        y = hflat[:, 1024:2048]
        gated = hflat[:, 2048:3072].rearrange("p (t e s) -> p (t e) s", t=TT, e=QUAD)
        sil = hflat[:, 3072:3328].rearrange("p (f s) -> p f s", f=FC)
        hidf = hflat[:, 3328:3584].rearrange("p (f s) -> p f s", f=FC)
        gates = hflat[:, 3584:3840].rearrange("p (e s) -> p e s", e=QUAD)

        PS = ctx.enter_context(nc.psum_tensor("PS", [P, 8 * BANK], F32))

        def bank(b, lo=0, hi=BANK):
            return PS[:, b * BANK + lo:b * BANK + hi]

        bank_full = [sem(f"bank_full{b}") for b in range(8)]
        bank_read = [sem(f"bank_read{b}") for b in range(8)]
        ring_ld = [sem(f"ring_ld{i}") for i in range(RING)]
        s_const = sem("s_const")
        s_constp = sem("s_constp")
        s_xld = sem("s_xld")
        s_mld = sem("s_mld")
        s_vld = sem("s_vld")
        s_gld = sem("s_gld")
        s_wr = sem("s_wr")
        sq_ready = sem("sq_ready")
        diag_ready = sem("diag_ready")
        h_ready = sem("h_ready")
        xm_ready = sem("xm_ready")
        silu_ready = sem("silu_ready")
        conv_step = sem("conv_step")
        act_chain = sem("act_chain")
        dve_chain = sem("dve_chain")
        mrms_ready = sem("mrms_ready")
        mem_ready = sem("mem_ready")
        nm_ready = sem("nm_ready")
        p_ready = sem("p_ready")
        ln_ready = sem("ln_ready")
        bc_ready = sem("bc_ready")
        gdiff_ready = sem("gdiff_ready")
        gexp_ready = sem("gexp_ready")
        gstage_done = sem("gstage_done")
        inter_done = sem("inter_done")
        osq_ready = sem("osq_ready")
        rin_ready = sem("rin_ready")
        rex_ready = sem("rex_ready")
        mask_ready = sem("mask_ready")
        hhi_ready = sem("hhi_ready")
        cnt_ready = sem("cnt_ready")
        moe_done = sem("moe_done")
        s_out = sem("s_out")
        SEG = ("hi_ready", "lo_ready", "lo_ready_pool", "w_used", "onehot_ready", "gated_ready", "gu_read",
               "fold_full", "silu_done", "hid_step", "hid_ready", "y_half", "y_sum", "yhi_done", "ylo_done",
               "sc_full0", "sc_full1", "sc_read0", "sc_read1")
        seg = {(l, o): {x: sem(f"{x}_{l}{o}") for x in SEG} for l in range(DEPTH) for o in ("m", "o")}
        ov_ld = [[sem(f"ov_ld{l}_{i}") for i in range(RING)] for l in range(DEPTH)]
        ov_tables = [sem(f"ov_tables{l}") for l in range(DEPTH)]

        def full(key):
            b, k = plan.at[key]
            return bank_full[b], k + 1

        def read(key):
            b, k = plan.at[key]
            return bank_read[b], k + 1

        def vcol(name, i):
            return vecT[:, VROWS[name][0] + i:VROWS[name][0] + i + 1]

        norm_gain = [("norm_mix", 0), ("conv_ln_g", 0), ("norm_xattn", 0), ("norm_ffn", 0),
                     ("norm_mix", 8), ("norm_xattn", 8), ("norm_ffn", 8), ("norm_final", 0)]
        norm_key = [("xt",), None, ("co",), ("xo", 0), None, ("go",), ("xo", 1), None]
        norm_src = [cv if i == 1 else xT for i in range(8)]
        norm_dst = [cv if i == 1 else hT for i in range(8)]
        LAST = 7

        def norm_source(eng, i, c):
            if i == 2 and c == 0:
                eng.wait_ge(*full(("co", C - 1)))
            if norm_key[i] is not None:
                eng.wait_ge(*read(norm_key[i] + (c,)))
            elif i == 1:
                if c < C - 1:
                    eng.wait_ge(xm_ready, c + 1)
                else:
                    eng.wait_ge(*read(("mu",)))
            elif c == 0:
                eng.wait_ge(moe_done, 1 if i == 4 else 2)

        def wait_h(eng, i, c):
            eng.wait_ge(h_ready, C * i + c + 1)

        def up_part(Q, r, j):
            return (j, j % WB) if isinstance(Q, int) and Q == 0 and r == 0 else (48 * Q + 12 * r - 4 + j, (j - 4) % WB)

        def down_part(Q, r, j):
            return 48 * Q + 12 * r + 4 + j, (j + 4) % WB

        def on_pool(down, j):
            return j in (POOL_DOWN if down else POOL_UP)

        def lo_count(Q, r, down, j):
            pool_ = on_pool(down, j)

            def count(down, n):
                return sum(on_pool(down, i) == pool_ for i in range(n))

            e = 4 * Q + r
            if isinstance(Q, int) and e == 0:
                return count(False, j + 1)
            before = (count(False, 8) + count(True, PARTS)) * e - count(True, PARTS)
            return before + (count(False, 8) + count(True, j + 1) if down else count(False, j + 1))

        def tail_lo(e, j):
            return lo_count(0, e + 1, True, j) - sum(on_pool(False, i) == on_pool(True, j) for i in range(8))

        def tile_before(Q, r, i):
            return i if isinstance(Q, int) and Q == 0 and r == 0 else 12 * Q + 3 * r - 1 + i

        def small_uses(Q, k):
            return 5 + 14 * Q + k // 2

        def slot_of(n):
            return ring[:, n % RING, :]

        block = ctx.enter_context(nc.Block())

        @block.tensor
        def _(pe):
            def take(key, b=None):
                b, k = plan.use(key, b)
                if k:
                    pe.wait_ge(bank_read[b], k)
                return b

            def tile(l, kind, i, key):
                n = tile_no[(l, kind, i)]
                pe.wait_ge(ring_ld[n % RING], 16 * (n // RING + 1))
                release[n] = key
                return slot_of(n)

            def group(o, lhs, rhs, nk):
                for k in range(nk):
                    mm = pe.matmul(o, lhs(k), rhs(k), start=(k == 0), stop=(k == nk - 1))
                return mm

            def token_sums(key, src, wait, b=None):
                b = take(key, b)
                n = len(src)
                for c in range(n):
                    wait(c)
                    for t in range(TT):
                        mm = pe.matmul(bank(b, t, t + 1), src[c][:, t * P:(t + 1) * P], ones[:, 0:1],
                                       start=(c == 0 and t == 0), stop=(c == n - 1), skip_group_check=True)
                mm.then_inc(bank_full[b], 1)

            def spread_sums(key, src, wait):
                b = take(key)
                for c in range(C):
                    wait(c)
                    mm = pe.matmul(bank(b), ones[:, :], src[c], start=(c == 0), stop=(c == C - 1))
                mm.then_inc(bank_full[b], 1)

            diag = [0]

            def spread(key, b=None):
                b = take(key, b)
                for t in range(TT):
                    diag[0] += 1
                    pe.wait_ge(diag_ready, diag[0])
                    mm = pe.matmul(bank(b, t * P, (t + 1) * P), ones[:, :], dg[:, t, :], start=True, stop=True)
                mm.then_inc(bank_full[b], 1)

            def norm(i):
                spread_sums(("rms", i), [hT[:, c, :] for c in range(C)],
                            lambda c: pe.wait_ge(sq_ready, C * i + c + 1))

            def project(l, kind, i, key, src, wait=None):
                w = tile(l, kind, i, key + (4 * i + 3,))
                for m in range(4):
                    project_chunk(w, m, key + (4 * i + m,), src, wait if m == 0 else None)

            def project_chunk(w, m, key, src, wait=None):
                b = take(key)
                for k in range(C):
                    if wait is not None:
                        wait(k)
                    mm = pe.matmul(bank(b), w[:, k * 512 + m * P:k * 512 + (m + 1) * P], src[:, k, :],
                                   start=(k == 0), stop=(k == C - 1))
                mm.then_inc(bank_full[b], 1)

            def transposes(key, pairs):
                b = take(key)
                for j, src in enumerate(pairs):
                    mm = pe.transpose(bank(b, j * P, (j + 1) * P), src, ident[:, :])
                mm.then_inc(bank_full[b], 1)

            def mem_kv(l):
                for i in range(2):
                    w = tile(l, "kv", i, ("k", l, 2 * i + 1))
                    for jj in range(2):
                        b = take(("k", l, 2 * i + jj))
                        for m in (2 * jj, 2 * jj + 1):
                            mm = group(bank(b, (m % 2) * NMEM, (m % 2 + 1) * NMEM),
                                       lambda k: w[:, k * 512 + m * P:k * 512 + (m + 1) * P],
                                       lambda k: memT[:, k, :], C)
                        mm.then_inc(bank_full[b], 1)
                for i in range(2):
                    w = tile(l, "kv", 2 + i, ("v", l, i, 1))
                    for mt in range(2):
                        b = take(("v", l, i, mt))
                        group(bank(b), lambda k: memT[:, k, mt * P:(mt + 1) * P],
                              lambda k: w[:, k * 512:(k + 1) * 512], C).then_inc(bank_full[b], 1)

            def attention(l):
                def scores(h):
                    for c in (2 * h, 2 * h + 1):
                        pe.wait_ge(*read(("q", l, c)))
                    for sp in range(2):
                        b = take(("s", l, h, sp))
                        for st in range(2):
                            t = 2 * sp + st
                            mm = group(bank(b, st * NMEM, (st + 1) * NMEM),
                                       lambda j: qT[:, 2 * h + j, t * P:(t + 1) * P],
                                       lambda j: kT[:, 2 * h + j, :], 2)
                        mm.then_inc(bank_full[b], 1)

                def values(h):
                    pe.wait_ge(p_ready, 8 * l + 2 * h + 2)
                    for mc in range(2):
                        transposes(("pt", l, h, mc),
                                   [probs[:, (2 * h + t // 2) % 4, t % 2, mc * P:(mc + 1) * P] for t in range(TT)])
                    for mc in range(2):
                        pe.wait_ge(*read(("pt", l, h, mc)))
                    for c in (2 * h, 2 * h + 1):
                        b = take(("o", l, c))
                        group(bank(b), lambda mc: vM[:, mc, c * P:(c + 1) * P],
                              lambda mc: pT[:, h % 2, mc, :], 2).then_inc(bank_full[b], 1)

                ni = 2 if l == 0 else 5
                norm(ni)
                for i in range(2):
                    project(l, "xq", i, ("q", l), hT, (lambda k: wait_h(pe, ni, k)) if i == 0 else None)
                for j in range(4):
                    pe.wait_ge(*read(("k", l, j)))
                    pe.wait_ge(*read(("v", l, j // 2, j % 2)))
                scores(0)
                for h in range(HEADS):
                    if h + 1 < HEADS:
                        scores(h + 1)
                    values(h)
                for i in range(2):
                    project(l, "xo", i, ("xo", l), oT,
                            (lambda k: pe.wait_ge(*read(("o", l, k)))) if i == 0 else None)

            def moe_segment(l, o, nq):
                g = seg[(l, o)]
                base = moe_base[l] if o == "m" else 0
                ld = ring_ld if o == "m" else ov_ld[l]

                def small(Q, k):
                    b = k % 2
                    pe.wait_ge(g[f"sc_read{b}"], small_uses(Q, k))
                    return b

                def part(Q, r, down, j, lhs, banks):
                    n, buf = (down_part if down else up_part)(Q, r, j)
                    for w, s in ((whi, "hi_ready"), (wlo, "lo_ready_pool" if on_pool(down, j) else "lo_ready")):
                        pe.wait_ge(g[s], n + 1 if w is whi else lo_count(Q, r, down, j))
                        for m in range(2):
                            if down:
                                o_ = bank(banks[m])
                                k = j
                                x = lhs(j)
                                st, sp_ = (w is whi and j == 0), (w is wlo and j == 3)
                            else:
                                o_ = bank(banks[j // 4])
                                k = 2 * (j % 4) + m
                                x = lhs(k)
                                st, sp_ = (w is whi and k == 0), (w is wlo and k == C - 1)
                            mm = pe.matmul(o_, x, w[:, buf, m * 512:(m + 1) * 512], start=st, stop=sp_)
                    mm.then_inc(g["w_used"], 1)

                def up(Q, r):
                    first = isinstance(Q, int) and Q == 0 and r == 0
                    if not first:
                        pe.wait_ge(g["gu_read"], 2 * (4 * Q + r))
                    for j in range(8):
                        if r == 0 and j < PARTS:
                            for c in (2 * j, 2 * j + 1):
                                pe.wait_ge(g[f"sc_read{c % 2}"], c // 2 + 1 if first else 14 * Q - 3 + c // 2)
                        part(Q, r, False, j, lambda k: xg[:, k, r, :], (0, 1))

                def folded(Q, r):
                    e = 4 * Q + r
                    for half, src in ((0, graw), (1, uraw)):
                        pe.wait_ge(g["gu_read"], 2 * e + half + 1)
                        for f in range(FC):
                            mm = pe.matmul(bank(2 + half, f * P, (f + 1) * P), src[:, f * P:(f + 1) * P], fold[:, :],
                                           start=True, stop=True)
                        mm.then_inc(g["fold_full"], 1)

                def down(Q, r, tail=False):
                    e = 4 * Q + r - 1
                    pe.wait_ge(g["hid_ready"], e + 1)
                    if not (isinstance(Q, int) and e == 0):
                        pe.wait_ge(g["y_sum"], e)
                    for j in range(PARTS):
                        if tail:
                            n = 48 * Q + 12 * (r - 1) + 8 + j
                            buf = (j - 4) % WB
                            for w in (whi, wlo):
                                sname = "hi_ready" if w is whi else ("lo_ready_pool" if on_pool(True, j) else "lo_ready")
                                cnt = n + 1 if w is whi else tail_lo(e, j)
                                pe.wait_ge(g[sname], cnt)
                                for m in range(2):
                                    mm = pe.matmul(bank(4 + m), hid[:, j, :], w[:, buf, m * 512:(m + 1) * 512],
                                                   start=(w is whi and j == 0), stop=(w is wlo and j == 3))
                            mm.then_inc(g["w_used"], 1)
                        else:
                            part(Q, r, True, j, lambda f: hid[:, f, :], (4, 5))

                def one_hot_T(Q, pair, k):
                    b = small(Q, k)
                    for t in range(TT):
                        mm = pe.matmul(bank(6 + b, t * P, (t + 1) * P), onehot[:, t, pair * P:(pair + 1) * P],
                                       identR[:, :], start=True, stop=True)
                    mm.then_inc(g[f"sc_full{b}"], 1)

                def scatter(Q, pair, k0):
                    pe.wait_ge(g[f"sc_read{pair}"], 14 * Q + (10 if pair else 6))
                    pe.wait_ge(g["ylo_done"], 2 * Q + pair + 1)
                    for c in range(C):
                        b = small(Q, k0 + c)
                        for w in (yhi, ylo):
                            mm = pe.matmul(bank(6 + b), w[:, c * P:(c + 1) * P], onehotT[:, :],
                                           start=(w is yhi), stop=(w is ylo))
                        mm.then_inc(g[f"sc_full{b}"], 1)

                def gather(Q1, k0, Q):
                    first = Q is None
                    pe.wait_ge(g["onehot_ready"], Q1 + 1)
                    for c in range(C):
                        if first:
                            b = c % 2
                            if c >= 2:
                                pe.wait_ge(g[f"sc_read{b}"], c // 2)
                        else:
                            b = small(Q, k0 + c)
                        for p_, h in ((0, hhi), (1, hlo)):
                            for t in range(TT):
                                mm = pe.matmul(bank(6 + b, p_ * 256, (p_ + 1) * 256), h[:, t, c * P:(c + 1) * P],
                                               onehot[:, t, :], start=(t == 0), stop=(t == TT - 1))
                        mm.then_inc(g[f"sc_full{b}"], 1)
                    pe.wait_ge(g["gated_ready"], Q1 + 1)
                    for i in range(2):
                        if first:
                            b = i
                            pe.wait_ge(g[f"sc_read{b}"], 4)
                        else:
                            b = small(Q, k0 + C + i)
                        for t in range(TT):
                            mm = pe.matmul(bank(6 + b, 0, 2 * SL), ones[:, :],
                                           gated[:, t * QUAD + 2 * i:t * QUAD + 2 * i + 2, :], start=(t == 0),
                                           stop=(t == TT - 1))
                        mm.then_inc(g[f"sc_full{b}"], 1)

                def quad(Q, first, last):
                    up(Q, 0)
                    if not first:
                        down(Q, 0)
                    folded(Q, 0)
                    up(Q, 1)
                    if not first:
                        scatter(Q - 1, 1, 20)
                    down(Q, 1)
                    folded(Q, 1)
                    up(Q, 2)
                    one_hot_T(Q, 0, 0)
                    down(Q, 2)
                    folded(Q, 2)
                    up(Q, 3)
                    scatter(Q, 0, 1)
                    one_hot_T(Q, 1, 9)
                    down(Q, 3)
                    folded(Q, 3)
                    if not last:
                        gather(Q + 1, 10, Q)

                gather(0, 0, None)
                quad(0, True, False)
                with pe.Fori(1, nq - 1) as Q:
                    quad(Q, False, False)
                quad(nq - 1, False, True)
                down(nq - 1, 4, tail=True)
                scatter(nq - 1, 1, 10)

            pe.wait_ge(s_constp, NCONST)
            pe.wait_ge(s_xld, 16)
            for c in range(C):
                transposes(("xt", c), [x_tm[:, t, c * P:(c + 1) * P] for t in range(TT)])
            pe.wait_ge(s_vld, 16 * 14)
            b = take(("vt",))
            pe.transpose(bank(b, 0, NVEC), vrows[0:NVEC, 0:P], ident[0:NVEC, 0:NVEC])
            for j in (1, 2):
                mm = pe.transpose(bank(b, j * P, j * P + WDW_ROWS), vrows[0:WDW_ROWS, j * P:(j + 1) * P],
                                  ident[0:WDW_ROWS, 0:WDW_ROWS])
            mm.then_inc(bank_full[b], 1)
            norm(0)
            for half in range(2):
                wa = tile(0, "conv_in", half, ("a", 4 * half + 3))
                wg = tile(0, "conv_in", 2 + half, ("g", 4 * half + 3))
                for m in range(4):
                    c = 4 * half + m
                    project_chunk(wa, m, ("a", c), hT, (lambda k: wait_h(pe, 0, k)) if c == 0 else None)
                    project_chunk(wg, m, ("g", c), hT)
            pe.wait_ge(mem_ready, 2)
            for j in range(4):
                transposes(("mt", j), [mem_tm[:, mt, c * P:(c + 1) * P] for c in (2 * j, 2 * j + 1) for mt in range(2)])
            for j in range(4):
                pe.wait_ge(*read(("mt", j)))
            mem_kv(0)
            spread_sums(("mu",), [cv[:, c, :] for c in range(C)],
                        lambda c: pe.wait_ge(conv_step, 2 * KW * (c // 2 + 1)))
            norm(1)
            for i in range(2):
                project(0, "conv_out", i, ("co",), hT, (lambda k: pe.wait_ge(silu_ready, k + 1)) if i == 0 else None)
            attention(0)

            def moe(l):
                ni = 3 + 3 * l
                norm(ni)
                b = take(("lg", l))
                pe.wait_ge(s_wr, 64 * (l + 1))
                for c in range(C):
                    wait_h(pe, ni, c)
                for t in range(TT):
                    o = bank(b, t * (NG + NE), (t + 1) * (NG + NE))
                    for k in range(C):
                        pe.matmul(o, hT[:, k, t * P:(t + 1) * P], wr[:, k, :], start=(k == 0), stop=False)
                    mm = pe.matmul(o, ones[0:1, :], brow[0:1, :], start=False, stop=True)
                mm.then_inc(bank_full[b], 1)
                for t in range(TT):
                    for half in range(2):
                        transposes(("ht", l, t, half),
                                   [hT[:, 4 * half + j, t * P:(t + 1) * P] for j in range(4)])
                b = take(("cs", l))
                pe.wait_ge(mask_ready, l + 1)
                mk = rt[:, 0:TT * NE].rearrange("p (t e) -> p t e", t=TT)
                for t in range(TT):
                    for s in range(t + 1):
                        pe.matmul(bank(b, t * NE, (t + 1) * NE), (tri if s == t else ones)[:, :], mk[:, s, :],
                                  start=(s == 0), stop=(s == t))
                group(bank(b, TT * NE, (TT + 1) * NE), lambda s: ones[:, :], lambda s: mk[:, s, :],
                      TT).then_inc(bank_full[b], 1)
                for b in range(8):
                    pe.wait_ge(bank_read[b], plan.uses[b])
                moe_segment(l, "m", NQ)
                pe.wait_ge(cnt_ready, l + 1)
                worst = pe.value_load(cnt_i[0:1, l:l + 1], min_val=0, max_val=T)
                with pe.If(worst > SL):
                    for b in range(2):
                        pe.wait_ge(seg[(l, "m")][f"sc_read{b}"], 14 * NQ)
                    moe_segment(l, "o", (ROUNDS - 1) * NQ)

            moe(0)
            norm(4)
            project(1, "gla_in", 0, ("gq",), hT, lambda k: wait_h(pe, 4, k))
            project(1, "gla_in", 1, ("gq",), hT)
            pe.wait_ge(s_gld, 32)
            b = take(("alr",))
            group(PS[0:RANK, b * BANK:(b + 1) * BANK], lambda k: walr[:, k, :], lambda k: hT[:, k, :],
                  C).then_inc(bank_full[b], 1)
            pe.wait_ge(*read(("alr",)))
            for h in range(HEADS):
                b = take(("z", h))
                pe.matmul(bank(b), wa2[:, h * DK:(h + 1) * DK], alr, start=True, stop=True).then_inc(bank_full[b], 1)
            for half in range(2):
                w = tile(1, "gla_v", half, ("gv", half, TT - 1))
                for t in range(TT):
                    b = take(("gv", half, t))
                    group(bank(b), lambda k: hT[:, k, t * P:(t + 1) * P],
                          lambda k: w[:, k * 512:(k + 1) * 512], C).then_inc(bank_full[b], 1)
            for i in range(2):
                project(1, "gla_r", i, ("gr",), hT)
            for b in range(8):
                pe.wait_ge(bank_read[b], plan.uses[b])

            def gla_norm(h):
                token_sums(("gs", h), [EB[:, j, :] for j in range(2)],
                           lambda j: pe.wait_ge(osq_ready, 2 * h + j + 1), b=2)
                spread(("gb", h), b=3)

            for h in range(HEADS):
                pe.wait_ge(gstage_done, h + 1)
                b = take(("att", h), 2)
                for t in range(TT):
                    mm = pe.matmul(bank(b, t * P, (t + 1) * P), qT[:, 4 + h, t * P:(t + 1) * P],
                                   qT[:, h, t * P:(t + 1) * P], start=True, stop=True)
                mm.then_inc(bank_full[b], 1)
                b = take(("kd", h), 3)
                for t in range(TT):
                    mm = pe.transpose(bank(b, t * P, (t + 1) * P), hT[:, 4 + h, t * P:(t + 1) * P], ident[:, :])
                mm.then_inc(bank_full[b], 1)
                ob = (0, 1) if h % 2 == 0 else (6, 7)

                def update(c):
                    b = take(("u", h, c), 4 + c % 2)
                    lo, t = CH * (c % 2), c // 2
                    pe.matmul(bank(b, 0, 256), R5[lo:lo + CH, h * T + t * P:h * T + (t + 1) * P],
                              vG[lo:lo + CH, t, h * 256:(h + 1) * 256], start=True,
                              stop=True).then_inc(bank_full[b], 1)

                pe.wait_ge(*read(("kd", h)))
                update(0)
                update(1)
                if h:
                    gla_norm(h - 1)
                pe.wait_ge(*read(("att", h)))
                for j in range(2):
                    take(("go_ps", h, j), ob[j])
                for t in range(TT):
                    for j in range(2):
                        pe.matmul(bank(ob[j], t * P, (t + 1) * P), vG[:, t, h * 256 + j * P:h * 256 + (j + 1) * P],
                                  AT[:, t, :], start=True, stop=False, skip_group_check=True)
                    for c in (2 * t, 2 * t + 1):
                        if c == 0:
                            continue
                        pe.wait_ge(*read(("u", h, c - 1)))
                        for j in range(2):
                            mm = pe.matmul(bank(ob[j], c * CH, (c + 1) * CH), SS[:, c % 2, j * P:(j + 1) * P],
                                           hT[:, h, c * CH:(c + 1) * CH], start=False, stop=True,
                                           skip_group_check=True)
                            if c == NCH - 1:
                                mm.then_inc(bank_full[ob[j]], 1)
                        if c <= NCH - 3:
                            mm.then_inc(inter_done, 1)
                    for c in (2 * t + 2, 2 * t + 3):
                        if c < NCH - 1:
                            update(c)
            gla_norm(HEADS - 1)
            for i in range(2):
                project(1, "gla_o", i, ("go",), rG,
                        (lambda k: pe.wait_ge(*read(("go_ps", k // 2, k % 2)))) if i == 0 else None)
            mem_kv(1)
            attention(1)
            moe(1)
            norm(LAST)
            for c in range(C):
                wait_h(pe, LAST, c)
            for t in range(TT):
                for half in range(2):
                    transposes(("out", t, half), [hT[:, 4 * half + j, t * P:(t + 1) * P] for j in range(4)])

        @block.sync
        def _(sp):
            def dram(l, kind, i):
                cols = slice(i * 512, (i + 1) * 512)
                if kind == "conv_in":
                    w = a["conv_w_in"][0][:, cols]
                elif kind == "conv_out":
                    w = a["conv_w_out"][0][:, cols]
                elif kind == "kv":
                    w = a["xa_w_kv"][l][:, cols]
                elif kind == "xq":
                    w = a["xa_w_q"][l][:, cols]
                elif kind == "xo":
                    w = a["xa_w_o"][l][:, cols]
                elif kind == "gla_o":
                    w = a["gla_w_o"][0][:, cols]
                else:
                    first = {"gla_in": 0, "gla_v": 1024, "gla_r": 2048 + RANK}[kind] + i * 512
                    w = a["gla_w_in"][0][:, first:first + 512]
                return w.rearrange("(k p) n -> p k n", p=P)

            def dst(n, nk):
                return slot_of(n).rearrange("p (k n) -> p k n", k=nk)

            def expert(l, e, i):
                w = a[("moe_w_gate", "moe_w_up", "moe_w_down")[i]][l, e]
                return w.rearrange("(k p) n -> p k n", p=P)

            def quad_tiles(l, g, ld, base, Q, ex, first, before):
                for r in range(QUAD):
                    for i in range(3):
                        if i == 2 and first and r == 0:
                            continue
                        e = ex + r if i < 2 else (before if r == 0 else ex + r - 1)
                        n = tile_before(Q, r, i)
                        static = base + (n if first else 12 * 0 + 3 * r - 1 + i)
                        slot = static % RING
                        if not (first and n < RING):
                            sp.wait_ge(g["w_used"], 4 * (n - RING + 1))
                        elif g is seg[(l, "m")]:
                            sp.wait_ge(*full(release[base + n - RING]))
                        nk = C if i < 2 else FC
                        sp.dma_start(dst(slot, nk), expert(l, e, i)).then_inc(ld[slot], 16)

            def last_tile(l, g, ld, base, nq):
                n = 12 * nq - 1
                sp.wait_ge(g["w_used"], 4 * (n - RING + 1))
                slot = (base + n) % RING
                sp.dma_start(dst(slot, FC), expert(l, NE - 1, 2)).then_inc(ld[slot], 16)

            for name, (r0, rows) in VROWS.items():
                v = a[name]
                v = v.rearrange("(c p) -> c p", p=P) if len(v.shape) == 1 else v.rearrange("l (c p) -> (l c) p", p=P)
                sp.dma_start(vrows[r0:r0 + rows, 0:P], v).then_inc(s_vld, 16)
            w = a["conv_w_dw"][0].rearrange("k (c p) -> (k c) p", p=P)
            for j in range(2):
                sp.dma_start(vrows[0:WDW_ROWS, (j + 1) * P:(j + 2) * P],
                               w[j * WDW_ROWS:(j + 1) * WDW_ROWS, :]).then_inc(s_vld, 16)
            for l in range(DEPTH):
                main, over = seg[(l, "m")], seg[(l, "o")]
                for t in tiles[l]:
                    n = tile_no[(l,) + t]
                    if n - RING in release:
                        sp.wait_ge(*full(release[n - RING]))
                    elif n >= RING:
                        sp.wait_ge(seg[(l - 1, "m")]["w_used"], 4 * (n - RING + 1 - moe_base[l - 1]))
                    sp.dma_start(dst(n, C), dram(l, *t)).then_inc(ring_ld[n % RING], 16)
                base = moe_base[l]
                quad_tiles(l, main, ring_ld, base, 0, 0, True, None)
                with sp.Fori(1, NQ) as Q:
                    quad_tiles(l, main, ring_ld, base, Q, 4 * Q, False, 4 * Q - 1)
                last_tile(l, main, ring_ld, base, NQ)
                sp.wait_ge(cnt_ready, l + 1)
                worst = sp.value_load(cnt_i[0:1, l:l + 1], min_val=0, max_val=T)
                with sp.If(worst > SL):
                    sp.wait_ge(main["w_used"], 4 * 3 * NE)
                    quad_tiles(l, over, ov_ld[l], 0, 0, 0, True, None)
                    with sp.Fori(1, NQ) as Q:
                        quad_tiles(l, over, ov_ld[l], 0, Q, 4 * Q, False, 4 * Q - 1)
                    with sp.Fori(1, ROUNDS - 1) as rd:
                        quad_tiles(l, over, ov_ld[l], 0, NQ * rd, 0, False, NE - 1)
                        with sp.Fori(1, NQ) as Q:
                            quad_tiles(l, over, ov_ld[l], 0, NQ * rd + Q, 4 * Q, False, 4 * Q - 1)
                    last_tile(l, over, ov_ld[l], 0, (ROUNDS - 1) * NQ)
                    sp.wait_ge(over["w_used"], 4 * 3 * NE * (ROUNDS - 1))
            o_dram = out.rearrange("b (t p) d -> (b t) p d", p=P)
            for t in range(TT):
                for half in range(2):
                    sp.wait_ge(*read(("out", t, half)))
                sp.dma_start(o_dram[t], x_tm[:, t, :]).then_inc(s_out, 16)
            sp.wait_ge(s_out, 16 * TT)

        @block.gpsimd
        def _(pool):
            def moe_pool(l, o, nq):
                g = seg[(l, o)]
                base = moe_base[l] if o == "m" else 0

                def low(n, buf, slot, j):
                    pool.wait_ge(g["hi_ready"], n + 1)
                    pool.tensor_tensor(wlo[:, buf, :], ring[:, slot, j * PW:(j + 1) * PW], whi[:, buf, :].bitcast(F32),
                                       ALU.subtract).then_inc(g["lo_ready_pool"], 1)

                def low_part(Q, r, down, j, first):
                    n, buf = (down_part if down else up_part)(Q, r, j)
                    i = 2 if down else j // 4
                    t0 = tile_before(0, 0, i) if first and r == 0 else 3 * r - 1 + i
                    low(n, buf, (base + t0) % RING, j % 4)

                def y_low(count):
                    pool.wait_ge(g["yhi_done"], count)
                    pool.tensor_tensor(ylo[:, :], y, yhi[:, :].bitcast(F32), ALU.subtract).then_inc(g["ylo_done"], 1)

                def quad(Q, first):
                    for r in range(QUAD):
                        for j in POOL_UP:
                            low_part(Q, r, False, j, first)
                            if j == POOL_UP[0] and r == 1 and not first:
                                y_low(2 * Q)
                            if j == POOL_UP[0] and r == 3:
                                y_low(2 * Q + 1)
                        if not (first and r == 0):
                            for j in POOL_DOWN:
                                low_part(Q, r, True, j, first)

                quad(0, True)
                with pool.Fori(1, nq) as Q:
                    quad(Q, False)
                for j in POOL_DOWN:
                    low(48 * nq - 4 + j, (j - 4) % WB, (base + 12 * nq - 1) % RING, j)
                y_low(2 * nq)

            pool.memset(ident[:, :], 0.0).then_inc(s_constp, 1)
            pool.memset(ones[:, :], 1.0).then_inc(s_constp, 1)
            pool.memset(tri[:, :], 1.0).then_inc(s_constp, 1)
            pool.memset(gmask[:, :], 1.0).then_inc(s_constp, 1)
            pool.memset(fold[:, :], 0.0).then_inc(s_constp, 1)
            pool.wait_ge(s_constp, 5)
            pool.affine_select(out=ident[:, :], in_=ident[:, :], compare_op=ALU.not_equal, fill=1.0, base=0,
                               pattern=[[-1, P]], channel_multiplier=1).then_inc(s_constp, 1)
            pool.affine_select(out=tri[:, :], in_=tri[:, :], compare_op=ALU.is_gt, fill=0.0, base=0,
                               pattern=[[1, P]], channel_multiplier=-1).then_inc(s_constp, 1)
            pool.affine_select(out=gmask[:, :], in_=gmask[:, :], compare_op=ALU.is_ge, fill=0.0, base=0,
                               pattern=[[1, P]], channel_multiplier=-1).then_inc(s_constp, 1)
            for i, off in enumerate((-SL, 0, SL)):
                if i:
                    pool.wait_ge(s_constp, 8 + i)
                pool.affine_select(out=fold[:, :], in_=fold[:, :], compare_op=ALU.not_equal, fill=1.0, base=off,
                                   pattern=[[-1, P]], channel_multiplier=1).then_inc(s_constp, 1)
            pool.wait_ge(s_constp, 11)
            pool.memset(gmask[0:CH, CH:P], 0.0).then_inc(s_constp, 1)
            pool.iota(iota[:, :], pattern=[[1, SL]], base=0, channel_multiplier=0,
                      allow_small_or_imprecise_dtypes=True).then_inc(s_constp, 1)
            for l in range(DEPTH):
                if l == 1:
                    pool.wait_ge(moe_done, 1)
                    with nc.allow_non_contiguous_dma(reason="16 columns of a wide matrix"):
                        pool.dma_start(walr, a["gla_w_in"][0][:, 2048:2048 + RANK].rearrange("(k p) n -> p k n", p=P)
                                       ).then_inc(s_gld, 16)
                    pool.dma_start(wa2, a["gla_w_a2"][0]).then_inc(s_gld, 16)
                for c in range(C):
                    pool.wait_ge(*read(("xo", l, c)))
                ws = [(wr[:, :, 0:NG], a["moe_w_grp"][l].rearrange("(k p) n -> p k n", p=P)),
                      (wr[:, :, NG:], a["moe_w_exp"][l].rearrange("(k p) n -> p k n", p=P)),
                      (brow[:, 0:NG], a["moe_b_grp"][l:l + 1, :]), (brow[:, NG:], a["moe_b_exp"][l:l + 1, :])]
                for d, s in ws:
                    pool.dma_start(d, s).then_inc(s_wr, 16)
                moe_pool(l, "m", NQ)
                pool.wait_ge(cnt_ready, l + 1)
                worst = pool.value_load(cnt_i[0:1, l:l + 1], min_val=0, max_val=T)
                with pool.If(worst > SL):
                    moe_pool(l, "o", (ROUNDS - 1) * NQ)

        @block.scalar
        def _(act):
            chain = [0]

            def link(ins):
                chain[0] += 1
                ins.then_inc(act_chain, 1)
                act.wait_ge(act_chain, chain[0])

            def evacuate(key, dst, scale=1.0, lo=0, hi=BANK):
                act.wait_ge(*full(key))
                b = plan.at[key][0]
                act.activation(dst, bank(b, lo, hi), ACT.Copy, scale=scale).then_inc(bank_read[b], 1)

            def norm(i):
                for c in range(C):
                    norm_source(act, i, c)
                    act.activation(hT[:, c, :], norm_src[i][:, c, :], ACT.Square).then_inc(sq_ready, 1)
                act.wait_ge(*full(("rms", i)))
                b = plan.at[("rms", i)][0]
                act.activation(rms, bank(b), ACT.Sqrt, bias=EPS, scale=1.0 / D).then_inc(bank_read[b], 1)

            def mem_kv(l):
                for j in range(4):
                    evacuate(("k", l, j), RK[:, j * 512:(j + 1) * 512])
                for i in range(2):
                    for mt in range(2):
                        evacuate(("v", l, i, mt), vM[:, mt, i * 512:(i + 1) * 512])

            def attention(l):
                def softmax(h):
                    if h >= 2:
                        act.wait_ge(*full(("pt", l, h - 2, 1)))
                    for sp in range(2):
                        unit = 2 * h + sp
                        act.wait_ge(nm_ready, 8 * l + unit + 1)
                        b = plan.at[("s", l, h, sp)][0]
                        for st in range(2):
                            col = 2 * unit + st
                            ins = act.activation(probs[:, unit % 4, st, :], bank(b, st * NMEM, (st + 1) * NMEM), ACT.Exp,
                                                 bias=nmaxs[:, col:col + 1], scale=1.0 / 16.0,
                                                 accum_out=ssum[:, col:col + 1])
                        ins.then_inc(bank_read[b], 1)

                norm(2 if l == 0 else 5)
                for c in range(C):
                    evacuate(("q", l, c), qT[:, c, :])
                for c in (7,):
                    act.wait_ge(*full(("q", l, c)))
                softmax(0)
                for h in range(HEADS):
                    if h + 1 < HEADS:
                        softmax(h + 1)
                    if h >= 2:
                        act.wait_ge(*full(("o", l, 2 * (h - 2) + 1)))
                    for mc in range(2):
                        evacuate(("pt", l, h, mc), pT[:, h % 2, mc, :])

            def moe_segment(l, o, nq):
                g = seg[(l, o)]
                base = moe_base[l] if o == "m" else 0
                ld = ring_ld if o == "m" else ov_ld[l]

                def high(n, buf, tile, Q, j, guard=True):
                    if j == 0:
                        count = (base + tile) // RING + 1
                        act.wait_ge(ld[(base + tile) % RING], 16 * count + 48 * Q)
                    if guard:
                        act.wait_ge(g["w_used"], n - WB + 1)
                    act.activation(whi[:, buf, :], ring[:, (base + tile) % RING, j * PW:(j + 1) * PW],
                                   ACT.Copy).then_inc(g["hi_ready"], 1)

                def high_up(Q, r, js):
                    first = isinstance(Q, int) and Q == 0 and r == 0
                    for j in js:
                        n, buf = up_part(Q, r, j)
                        i = j // 4
                        high(n, buf, i if first else 3 * r - 1 + i, Q, j % 4, guard=not (first and j < WB))

                def high_down(Q, r, js):
                    for j in js:
                        n, buf = down_part(Q, r, j)
                        high(n, buf, 3 * r + 1, Q, j)

                def take_gate_up(Q, r):
                    for half, d in ((0, graw), (1, uraw)):
                        act.wait_ge(g["w_used"], up_part(Q, r, 4 * half + 3)[0] + 1)
                        act.activation(d, bank(half), ACT.Copy).then_inc(g["gu_read"], 1)

                def silu(Q, r):
                    act.wait_ge(g["fold_full"], 2 * (4 * Q + r) + 2)
                    act.activation(sil, bank(2).rearrange("p (f s) -> p f s", f=FC)[:, :, 0:SL],
                                   ACT.Silu).then_inc(g["silu_done"], 1)

                def half_y(Q, r, first=False):
                    act.wait_ge(g["w_used"], 48 * Q if r == 0 and isinstance(Q, int) and Q == nq
                                else down_part(Q, r, 3)[0] + 1)
                    if (r - 1) % 2 == 0:
                        if not first:
                            act.wait_ge(g["ylo_done"], 2 * Q + r // 2)
                        ins = act.activation(y[0:SL, :], PS[SL:P, 4 * BANK:6 * BANK], ACT.Copy)
                    else:
                        ins = act.activation(y[SL:P, :], PS[0:SL, 4 * BANK:6 * BANK], ACT.Copy)
                    ins.then_inc(g["y_half"], 1)

                def take_x(n0):
                    for c in range(C):
                        b = c % 2
                        act.wait_ge(g[f"sc_full{b}"], n0 + c // 2 + 1)
                        act.activation(xg[:, c, :, :].rearrange("p e (h s) -> p h e s", h=2),
                                       bank(6 + b).rearrange("p (h e s) -> p h e s", h=2, e=QUAD), ACT.Copy
                                       ).then_inc(g[f"sc_read{b}"], 1)

                def quad(Q, first, last):
                    for r in range(QUAD):
                        e0 = first and r == 0
                        high_up(Q, r, range(WB if e0 else AHEAD, 8))
                        if not e0:
                            high_down(Q, r, (0, 1, 2))
                        take_gate_up(Q, r)
                        if not e0:
                            high_down(Q, r, (3,))
                        end = last and r == QUAD - 1
                        if not end:
                            high_up(Q + (r + 1) // 4, (r + 1) % 4, range(AHEAD))
                        else:
                            for j in (0, 1):
                                high(48 * nq - 4 + j, (j - 4) % WB, 12 * nq - 1, 0, j)
                        if not e0:
                            half_y(Q, r, first and r == 1)
                        silu(Q, r)
                        if r == QUAD - 1 and not last:
                            take_x(small_uses(Q, 10))

                high_up(0, 0, range(WB))
                take_x(0)
                quad(0, True, False)
                with act.Fori(1, nq - 1) as Q:
                    quad(Q, False, False)
                quad(nq - 1, False, True)
                for j in (2, 3):
                    high(48 * nq - 4 + j, (j - 4) % WB, 12 * nq - 1, 0, j)
                half_y(nq, 0)

            def moe(l):
                norm(3 + 3 * l)
                for t in range(TT):
                    for half in range(2):
                        act.wait_ge(*full(("ht", l, t, half)))
                        b = plan.at[("ht", l, t, half)][0]
                        act.activation(hhi[:, t, half * 512:(half + 1) * 512], bank(b), ACT.Copy).then_inc(hhi_ready, 1)
                    if t == 0:
                        act.wait_ge(rin_ready, 2 * l + 1)
                        act.activation(rt[:, 576:592], rt[:, 560:576], ACT.Exp).then_inc(rex_ready, 1)
                    if t == 1:
                        act.wait_ge(rin_ready, 2 * l + 2)
                        act.activation(rt[:, 604:608], rt[:, 600:604], ACT.Exp).then_inc(rex_ready, 1)
                moe_segment(l, "m", NQ)
                act.wait_ge(cnt_ready, l + 1)
                worst = act.value_load(cnt_i[0:1, l:l + 1], min_val=0, max_val=T)
                with act.If(worst > SL):
                    moe_segment(l, "o", (ROUNDS - 1) * NQ)

            act.dma_start(x_tm[:, :, :], a["x"].rearrange("b (t p) d -> p (b t) d", p=P)).then_inc(s_xld, 16)
            act.dma_start(mem_tm[:, :, :], a["mem"].rearrange("b (t p) d -> p (b t) d", p=P)).then_inc(s_mld, 16)
            for c in range(1, C, 2):
                evacuate(("xt", c), xT[:, c, :])
            norm(0)
            act.wait_ge(s_mld, 16)
            ebf = EB[:, :, :].rearrange("p a t -> p (a t)")
            for mt in range(2):
                link(act.activation(ebf, mem_tm[:, mt, :], ACT.Square, accum_out=mstat[:, mt:mt + 1]))
            act.activation(mstat, mstat, ACT.Sqrt, bias=EPS, scale=1.0 / D).then_inc(mrms_ready, 1)
            for c in range(C):
                act.wait_ge(*full(("g", c)))
                if c >= 2:
                    act.wait_ge(*read(("a", c - 2)))
                b = plan.at[("g", c)][0]
                act.activation(EB[:, c % 2, :], bank(b), ACT.Sigmoid,
                               bias=vcol("conv_b_in", 8 + c)).then_inc(bank_read[b], 1)
            mem_kv(0)
            norm(1)
            for c in range(C):
                wait_h(act, 1, c)
                act.activation(hT[:, c, :], cv[:, c, :], ACT.Silu, bias=vcol("conv_ln_b", c)).then_inc(silu_ready, 1)
            attention(0)
            moe(0)
            norm(4)
            for c in range(C):
                evacuate(("gq", c), qT[:, c, :], scale=float(DK) ** -0.5 if c < HEADS else 1.0)
            b = plan.at[("alr",)][0]
            act.wait_ge(*full(("alr",)))
            act.activation(alr, PS[0:RANK, b * BANK:(b + 1) * BANK], ACT.Copy).then_inc(bank_read[b], 1)
            for h in range(HEADS):
                act.wait_ge(*full(("z", h)))
                if h >= 2:
                    act.wait_ge(bc_ready, h - 1)
                e = EB[:, h % 2, :]
                link(act.activation(e, bank(plan.at[("z", h)][0]), ACT.Abs, bias=vcol("gla_b_a", h)))
                link(act.activation(e, e, ACT.Exp, scale=-1.0))
                act.activation(e, e, ACT.Ln, bias=1.0).then_inc(ln_ready, 1)
            for h in range(HEADS):
                act.wait_ge(gdiff_ready, 2 * h + 2)
                atf = AT[:, :, :].rearrange("p a t -> p (a t)")
                ssf = SS[:, :, :].rearrange("p a t -> p (a t)")
                r5 = R5[:, h * T:(h + 1) * T]
                act.activation(atf, EB[:, 0, :], ACT.Exp, scale=1.0 / TAU).then_inc(gexp_ready, 1)
                act.activation(ssf, EB[:, 0, :], ACT.Exp, scale=-1.0 / TAU).then_inc(gexp_ready, 1)
                act.activation(r5, r5, ACT.Exp, scale=1.0 / TAU).then_inc(gexp_ready, 1)
                act.activation(EB[:, 1, :], EB[:, 1, :], ACT.Exp, scale=1.0 / TAU).then_inc(gexp_ready, 1)
            for c in range(C):
                act.wait_ge(*full(("gr", c)))
                b = plan.at[("gr", c)][0]
                act.activation(rG[:, c, :], bank(b), ACT.Silu).then_inc(bank_read[b], 1)

            def gla_norm(h):
                for j in range(2):
                    act.wait_ge(*full(("go_ps", h, j)))
                    if h == 0:
                        act.wait_ge(gstage_done, HEADS)
                    act.activation(EB[:, j, :], bank(plan.at[("go_ps", h, j)][0]), ACT.Square).then_inc(osq_ready, 1)
                act.wait_ge(*full(("gs", h)))
                b = plan.at[("gs", h)][0]
                act.activation(rstat, bank(b, 0, TT), ACT.Sqrt, bias=EPS, scale=1.0 / 256.0).then_inc(bank_read[b], 1)

            for h in range(HEADS):
                evacuate(("kd", h), R5[:, h * T:(h + 1) * T])
                if h:
                    gla_norm(h - 1)
            gla_norm(HEADS - 1)
            mem_kv(1)
            attention(1)
            moe(1)
            norm(LAST)
            for t in range(TT):
                evacuate(("out", t, 1), x_tm[:, t, 512:1024])

        @block.vector
        def _(dve):
            chain = [0]

            def link(ins):
                chain[0] += 1
                ins.then_inc(dve_chain, 1)
                dve.wait_ge(dve_chain, chain[0])

            def evacuate(key, dst):
                dve.wait_ge(*full(key))
                b = plan.at[key][0]
                dve.tensor_copy(dst, bank(b)).then_inc(bank_read[b], 1)

            def diagonals(vals):
                for t in range(TT):
                    dve.tensor_scalar(dg[:, t, :], ident[:, :], vals[:, t:t + 1], None, ALU.mult).then_inc(diag_ready, 1)

            def norm(i):
                dve.wait_ge(*read(("rms", i)))
                link(dve.reciprocal(rms, rms))
                name, g0 = norm_gain[i]
                for c in range(C):
                    dve.scalar_tensor_tensor(norm_dst[i][:, c, :], norm_src[i][:, c, :], vcol(name, g0 + c), rms,
                                             ALU.mult, ALU.mult).then_inc(h_ready, 1)

            def residual(key, bias=None):
                for c in range(C):
                    dve.wait_ge(*full(key + (c,)))
                    b = plan.at[key + (c,)][0]
                    if bias is None:
                        ins = dve.tensor_tensor(xT[:, c, :], bank(b), xT[:, c, :], ALU.add)
                    else:
                        ins = dve.scalar_tensor_tensor(xT[:, c, :], bank(b), vcol(bias, c), xT[:, c, :],
                                                       ALU.add, ALU.add)
                    ins.then_inc(bank_read[b], 1)

            def attention(l):
                norm(2 if l == 0 else 5)

                def maxima(h):
                    for sp in range(2):
                        unit = 2 * h + sp
                        dve.wait_ge(*full(("s", l, h, sp)))
                        b = plan.at[("s", l, h, sp)][0]
                        cols = slice(2 * unit, 2 * unit + 2)
                        link(dve.tensor_reduce(nmax[:, cols], bank(b).rearrange("p (s m) -> p s m", s=2), AX.X, ALU.max))
                        dve.tensor_scalar(nmaxs[:, cols], nmax[:, cols], -1.0 / 16.0, None,
                                          ALU.mult).then_inc(nm_ready, 1)

                def normalise(h):
                    for sp in range(2):
                        unit = 2 * h + sp
                        dve.wait_ge(*read(("s", l, h, sp)))
                        cols = slice(2 * unit, 2 * unit + 2)
                        link(dve.reciprocal(srec[:, cols], ssum[:, cols]))
                        r = srec[:, cols].unsqueeze(2).to_broadcast([P, 2, NMEM])
                        dve.tensor_tensor(probs[:, unit % 4], probs[:, unit % 4], r, ALU.mult).then_inc(p_ready, 1)

                maxima(0)
                for h in range(HEADS):
                    normalise(h)
                    if h + 1 < HEADS:
                        maxima(h + 1)
                    for c in (2 * h, 2 * h + 1):
                        evacuate(("o", l, c), oT[:, c, :])
                residual(("xo", l))

            def router(l):
                W = NG + NE
                b = plan.at[("lg", l)][0]
                dve.wait_ge(*full(("lg", l)))
                dve.tensor_copy(lg[:, :, :], bank(b, 0, TT * W).rearrange("p (t w) -> p t w", t=TT)
                                ).then_inc(bank_read[b], 1)
                dve.wait_ge(*read(("lg", l)))
                gl = lg[:, :, 0:NG]
                el = lg[:, :, NG:W].rearrange("p t (g e) -> p t g e", g=NG)

                def v(o, n):
                    return rt[:, o:o + TT * n].rearrange("p (t n) -> p t n", t=TT)

                mask, mx, eq, idx = v(0, NE), v(128, 1), v(132, EG), v(164, 1)
                ohg, sel4, els = v(168, NG), v(184, NE), v(312, EG)
                oh1, oh2, m2, els2 = v(344, EG), v(376, EG), v(408, 1), v(412, EG)
                gv = v(444, EG)
                gin, gex, gsum, grec = v(560, NG), v(576, NG), v(592, 1), v(596, 1)
                din, dex, den = v(600, 1), v(604, 1), v(608, 1)

                def wide(x, n):
                    return x.to_broadcast([P, TT, n])

                def first_of(values, top, n, hot):
                    io = iota[:, 0:n].unsqueeze(1).to_broadcast([P, TT, n])
                    e = eq[:, :, 0:n]
                    link(dve.tensor_tensor(e, values, wide(top, n), ALU.is_equal))
                    link(dve.scalar_tensor_tensor(e, e, -float(EG), io, ALU.mult, ALU.add))
                    link(dve.tensor_reduce(idx, e, AX.X, ALU.min))
                    link(dve.tensor_scalar(idx, idx, float(EG), None, ALU.add))
                    link(dve.tensor_tensor(hot, io, wide(idx, n), ALU.is_equal))

                link(dve.tensor_reduce(mx, gl, AX.X, ALU.max))
                dve.tensor_tensor(gin, gl, wide(mx, NG), ALU.subtract).then_inc(rin_ready, 1)
                first_of(gl, mx, NG, ohg)
                for t in range(TT):
                    ins = dve.tensor_tensor(sel4[:, t, :].rearrange("p (g e) -> p g e", g=NG), el[:, t],
                                            ohg[:, t, :].unsqueeze(2).to_broadcast([P, NG, EG]), ALU.mult)
                    link(ins)
                for t in range(TT):
                    link(dve.tensor_reduce(els[:, t, :], sel4[:, t, :].rearrange("p (g e) -> p e g", g=NG),
                                           AX.X, ALU.add))
                link(dve.tensor_reduce(mx, els, AX.X, ALU.max))
                first_of(els, mx, EG, oh1)
                link(dve.scalar_tensor_tensor(els2, oh1, -BIG, els, ALU.mult, ALU.add))
                link(dve.tensor_reduce(m2, els2, AX.X, ALU.max))
                dve.tensor_tensor(din, m2, mx, ALU.subtract).then_inc(rin_ready, 1)
                first_of(els2, m2, EG, oh2)
                link(dve.tensor_tensor(els, oh1, oh2, ALU.add))
                for t in range(TT):
                    ins = dve.tensor_tensor(mask[:, t, :].rearrange("p (g e) -> p g e", g=NG),
                                            ohg[:, t, :].unsqueeze(2).to_broadcast([P, NG, EG]),
                                            els[:, t, :].unsqueeze(1).to_broadcast([P, NG, EG]), ALU.mult)
                    if t < TT - 1:
                        link(ins)
                    else:
                        ins.then_inc(mask_ready, 1)
                dve.wait_ge(rex_ready, 2 * l + 2)
                link(dve.tensor_reduce(gsum, gex, AX.X, ALU.add))
                link(dve.tensor_scalar(den, dex, 1.0, None, ALU.add))
                link(dve.tensor_tensor(gsum, gsum, den, ALU.mult))
                link(dve.reciprocal(grec, gsum))
                link(dve.tensor_tensor(gsum, grec, dex, ALU.mult))
                link(dve.tensor_tensor(oh1, oh1, wide(grec, EG), ALU.mult))
                link(dve.tensor_tensor(oh2, oh2, wide(gsum, EG), ALU.mult))
                link(dve.tensor_tensor(gv, oh1, oh2, ALU.add))
                for t in range(TT):
                    link(dve.tensor_tensor(sel4[:, t, :].rearrange("p (g e) -> p g e", g=NG),
                                           ohg[:, t, :].unsqueeze(2).to_broadcast([P, NG, EG]),
                                           gv[:, t, :].unsqueeze(1).to_broadcast([P, NG, EG]), ALU.mult))
                link(dve.tensor_copy(gtab[:, :, :].rearrange("p q (t e) -> p q t e", e=QUAD),
                                     sel4.rearrange("p t (q e) -> p q t e", e=QUAD)))
                b = plan.at[("cs", l)][0]
                for t in range(TT):
                    for half in range(2):
                        k = (l * TT + t) * 2 + half
                        dve.wait_ge(hhi_ready, k + 1)
                        bt = plan.at[("ht", l, t, half)][0]
                        cols = slice(half * 512, (half + 1) * 512)
                        dve.tensor_tensor(hlo[:, t, cols], bank(bt), hhi[:, t, cols].bitcast(F32),
                                          ALU.subtract).then_inc(bank_read[bt], 1)
                dve.wait_ge(*full(("cs", l)))
                dve.wait_ge(mask_ready, l + 1)
                link(dve.scalar_tensor_tensor(sel4, bank(b, 0, TT * NE).rearrange("p (t e) -> p t e", t=TT), 1.0, mask,
                                              ALU.add, ALU.mult))
                link(dve.tensor_scalar(ptab[:, :, :].rearrange("p q (t e) -> p q t e", e=QUAD),
                                       sel4.rearrange("p t (q e) -> p q t e", e=QUAD), -1.0, None, ALU.add))
                dve.tensor_reduce(maxc, bank(b, TT * NE, (TT + 1) * NE), AX.X, ALU.max).then_inc(bank_read[b], 1)
                dve.wait_ge(*read(("cs", l)))
                dve.tensor_copy(cnt_i[:, l:l + 1], maxc).then_inc(cnt_ready, 1)

            def moe_segment(l, o, nq):
                g = seg[(l, o)]
                base = moe_base[l] if o == "m" else 0

                def low(n, buf, tile, j):
                    dve.wait_ge(g["hi_ready"], n + 1)
                    dve.tensor_tensor(wlo[:, buf, :], ring[:, (base + tile) % RING, j * PW:(j + 1) * PW],
                                      whi[:, buf, :].bitcast(F32), ALU.subtract).then_inc(g["lo_ready"], 1)

                def low_up(Q, r, js):
                    first = isinstance(Q, int) and Q == 0 and r == 0
                    for j in js:
                        if not on_pool(False, j):
                            n, buf = up_part(Q, r, j)
                            low(n, buf, j // PARTS if first else 3 * r - 1 + j // PARTS, j % PARTS)

                def low_down(Q, r, js):
                    for j in js:
                        if not on_pool(True, j):
                            n, buf = down_part(Q, r, j)
                            low(n, buf, 3 * r + 1, j)

                def low_tail(js):
                    for j in js:
                        if not on_pool(True, j):
                            low(48 * nq - 4 + j, (j - 4) % WB, 12 * nq - 1, j)

                def make_onehot(i, col):
                    r = ptab[:, col, :].unsqueeze(2).to_broadcast([P, TT * QUAD, SL])
                    hot = onehot[:, :, :].rearrange("p t (e s) -> p (t e) s", e=QUAD)
                    dve.tensor_tensor(hot, iota[:, :].unsqueeze(1).to_broadcast([P, TT * QUAD, SL]), r,
                                      ALU.is_equal).then_inc(g["onehot_ready"], 1)
                    dve.wait_ge(g["onehot_ready"], i + 1)
                    gt = gtab[:, col, :].unsqueeze(2).to_broadcast([P, TT * QUAD, SL])
                    dve.tensor_tensor(gated, hot.bitcast(F32), gt, ALU.mult).then_inc(g["gated_ready"], 1)

                def next_round(count):
                    pf = ptab[:, :, :]
                    dve.tensor_scalar(pf, pf, -float(SL), None, ALU.add).then_inc(ov_tables[l], 1)
                    dve.wait_ge(ov_tables[l], count)

                def take_gates(n0):
                    for i in range(2):
                        dve.wait_ge(g[f"sc_full{i}"], n0 + 1)
                        dve.tensor_copy(gates[:, 2 * i:2 * i + 2, :],
                                        bank(6 + i, 0, 2 * SL).rearrange("p (e s) -> p e s", e=2)
                                        ).then_inc(g[f"sc_read{i}"], 1)

                def take_onehot_T(Q, k):
                    b = k % 2
                    dve.wait_ge(g[f"sc_full{b}"], small_uses(Q, k) + 1)
                    dve.tensor_copy(onehotT[:, :], bank(6 + b)).then_inc(g[f"sc_read{b}"], 1)

                def accumulate(Q, k0):
                    for c in range(C):
                        b = (k0 + c) % 2
                        dve.wait_ge(g[f"sc_full{b}"], small_uses(Q, k0 + c) + 1)
                        dve.tensor_tensor(xT[:, c, :], bank(6 + b), xT[:, c, :], ALU.add).then_inc(g[f"sc_read{b}"], 1)

                def hidden(Q, r):
                    e = 4 * Q + r
                    up_ = bank(3).rearrange("p (f s) -> p f s", f=FC)[:, :, 0:SL]
                    if r == 0:
                        for b in range(2):
                            dve.wait_ge(g[f"sc_read{b}"], 5 if isinstance(Q, int) and Q == 0 else 14 * Q + 1)
                    dve.wait_ge(g["silu_done"], e + 1)
                    dve.tensor_tensor(hidf, sil, up_, ALU.mult).then_inc(g["hid_step"], 1)
                    dve.wait_ge(g["hid_step"], 3 * e + 1)
                    dve.tensor_tensor(hidf, hidf, gates[:, r, :].unsqueeze(1).to_broadcast([P, FC, SL]),
                                      ALU.mult).then_inc(g["hid_step"], 1)
                    dve.wait_ge(g["hid_step"], 3 * e + 2)
                    dve.tensor_copy(hid[:, :, 0:SL], hidf).then_inc(g["hid_step"], 1)
                    dve.wait_ge(g["hid_step"], 3 * e + 3)
                    dve.tensor_tensor(hid[:, :, SL:], hidf, hid[:, :, 0:SL].bitcast(F32),
                                      ALU.subtract).then_inc(g["hid_ready"], 1)

                def add_y(Q, r):
                    lo = 0 if (r - 1) % 2 == 0 else SL
                    dve.wait_ge(g["y_half"], 4 * Q + r)
                    dve.tensor_tensor(y[lo:lo + SL, :], PS[lo:lo + SL, 4 * BANK:6 * BANK], y[lo:lo + SL, :],
                                      ALU.add).then_inc(g["y_sum"], 1)
                    if lo:
                        dve.wait_ge(g["y_sum"], 4 * Q + r)
                        dve.tensor_copy(yhi[:, :], y).then_inc(g["yhi_done"], 1)

                def quad(Q, first, last, col=None, round_=None):
                    for r in range(QUAD):
                        e0 = first and r == 0
                        low_up(Q, r, range(WB if e0 else AHEAD, 8))
                        if not e0:
                            low_down(Q, r, (0, 1))
                        if r == 1 and not first:
                            accumulate(Q - 1, 20)
                        if r == 2:
                            take_onehot_T(Q, 0)
                        if r == 3:
                            accumulate(Q, 1)
                            take_onehot_T(Q, 9)
                            if not last:
                                if round_ is not None:
                                    next_round(round_)
                                make_onehot(Q + 1, col)
                        if not e0:
                            low_down(Q, r, (2, 3))
                        if last and r == QUAD - 1:
                            low_tail((0, 1))
                        else:
                            low_up(Q + (r + 1) // QUAD, (r + 1) % QUAD, range(AHEAD))
                        if not e0:
                            add_y(Q, r)
                        hidden(Q, r)
                        if r == QUAD - 1 and not last:
                            take_gates(small_uses(Q, 18))

                over = o == "o"
                if over:
                    next_round(1)
                make_onehot(0, 0)
                low_up(0, 0, range(WB))
                take_gates(4)
                quad(0, True, False, 1)
                with dve.Fori(1, NQ - 1) as q:
                    quad(q, False, False, q + 1)
                if over:
                    quad(NQ - 1, False, False, 0, 2)
                    with dve.Fori(1, ROUNDS - 2) as rd:
                        with dve.Fori(0, NQ - 1) as q:
                            quad(NQ * rd + q, False, False, q + 1)
                        quad(NQ * rd + NQ - 1, False, False, 0, rd + 2)
                    with dve.Fori(0, NQ - 1) as q:
                        quad(NQ * (ROUNDS - 2) + q, False, False, q + 1)
                quad(nq - 1, False, True)
                low_tail((2, 3))
                add_y(nq, 0)
                accumulate(nq - 1, 10)
                for b in range(2):
                    dve.wait_ge(g[f"sc_read{b}"], 14 * nq)

            def moe(l):
                norm(3 + 3 * l)
                link(dve.tensor_copy(identR[:, :], ident[:, :]))
                router(l)
                moe_segment(l, "m", NQ)
                dve.wait_ge(cnt_ready, l + 1)
                worst = dve.value_load(cnt_i[0:1, l:l + 1], min_val=0, max_val=T)
                with dve.If(worst > SL):
                    moe_segment(l, "o", (ROUNDS - 1) * NQ)
                dve.memset(small[:, 130 + l:131 + l], 0.0).then_inc(moe_done, 1)

            dve.wait_ge(s_constp, NCONST)
            dve.memset(u[:, :, 0:KW - 1], 0.0).then_inc(s_const, 1)
            for c in range(0, C, 2):
                evacuate(("xt", c), xT[:, c, :])
            dve.wait_ge(*full(("vt",)))
            b = plan.at[("vt",)][0]
            dve.tensor_copy(vecT[:, :], bank(b, 0, NVEC))
            for j in range(2):
                ins = dve.tensor_copy(wdwT[:, j * WDW_ROWS:(j + 1) * WDW_ROWS],
                                      bank(b, (j + 1) * P, (j + 1) * P + WDW_ROWS))
            ins.then_inc(bank_read[b], 1)
            dve.wait_ge(*read(("vt",)))
            for c in range(C):
                dve.wait_ge(*read(("xt", c)))
            norm(0)
            dve.wait_ge(mrms_ready, 1)
            link(dve.reciprocal(mrec, mstat))
            for mt in range(2):
                dve.tensor_scalar(mem_tm[:, mt, :], mem_tm[:, mt, :], mrec[:, mt:mt + 1], None,
                                  ALU.mult).then_inc(mem_ready, 1)

            def glu(c):
                dve.wait_ge(*read(("g", c)))
                dve.wait_ge(*full(("a", c)))
                b = plan.at[("a", c)][0]
                dve.scalar_tensor_tensor(u[:, c, KW - 1:], bank(b), vcol("conv_b_in", c), EB[:, c % 2, :],
                                         ALU.add, ALU.mult).then_inc(bank_read[b], 1)

            def conv(c, k, step):
                if step >= 2:
                    dve.wait_ge(conv_step, step - 1)
                src = u[:, c, k:k + T]
                w = wdwT[:, k * C + c:k * C + c + 1]
                if k == 0:
                    ins = dve.tensor_scalar(cv[:, c, :], src, w, vcol("conv_b_dw", c), ALU.mult, ALU.add)
                else:
                    ins = dve.scalar_tensor_tensor(cv[:, c, :], src, w, cv[:, c, :], ALU.mult, ALU.add)
                ins.then_inc(conv_step, 1)

            dve.wait_ge(s_const, 1)
            step = 0
            for pair in range(C // 2):
                glu(2 * pair)
                glu(2 * pair + 1)
                for c in (2 * pair, 2 * pair + 1):
                    dve.wait_ge(*read(("a", c)))
                for k in range(KW):
                    for c in (2 * pair, 2 * pair + 1):
                        conv(c, k, step)
                        step += 1
                    if (pair, k) == (2, 20):
                      for j in range(4):
                        dve.wait_ge(*full(("mt", j)))
                        b = plan.at[("mt", j)][0]
                        for c in (2 * j, 2 * j + 1):
                            ins = dve.tensor_scalar(memT[:, c, :], bank(b, (c % 2) * NMEM, (c % 2 + 1) * NMEM),
                                                    vcol("norm_mem", c), None, ALU.mult)
                        ins.then_inc(bank_read[b], 1)
            dve.wait_ge(*full(("mu",)))
            b = plan.at[("mu",)][0]
            dve.wait_ge(conv_step, step)
            for c in range(C):
                dve.scalar_tensor_tensor(cv[:, c, :], bank(b), -1.0 / D, cv[:, c, :], ALU.mult,
                                         ALU.add).then_inc(xm_ready if c < C - 1 else bank_read[b], 1)
            dve.wait_ge(*read(("mu",)))
            norm(1)
            residual(("co",), "conv_b_out")
            for c in range(C):
                dve.wait_ge(*read(("co", c)))
            attention(0)
            for c in range(C):
                dve.wait_ge(*read(("xo", 0, c)))
            moe(0)
            norm(4)
            for h in range(HEADS):
                dve.wait_ge(ln_ready, h + 1)
                b = plan.at[("z", h)][0]
                r5 = R5[:, h * T:(h + 1) * T]
                dve.tensor_scalar(r5, bank(b), vcol("gla_b_a", h), 0.0, ALU.add, ALU.min).then_inc(bank_read[b], 1)
                dve.wait_ge(*read(("z", h)))
                link(dve.tensor_tensor(EB[:, h % 2, :], r5, EB[:, h % 2, :], ALU.subtract))
                for c in range(NCH):
                    sl = slice(c * CH, (c + 1) * CH)
                    ins = dve.tensor_tensor_scan(r5[:, sl], ones[:, 0:CH], EB[:, h % 2, sl], 0.0, ALU.mult, ALU.add)
                ins.then_inc(bc_ready, 1)
            for half in range(2):
                for t in range(TT):
                    evacuate(("gv", half, t), vG[:, t, half * 512:(half + 1) * 512])
            dve.wait_ge(bc_ready, HEADS)
            atf = AT[:, :, :].rearrange("p a t -> p (a t)")
            ssf = SS[:, :, :].rearrange("p a t -> p (a t)")
            for c in range(C):
                dve.wait_ge(*read(("gq", c)))
            dve.wait_ge(*full(("gr", C - 1)))
            for h in range(HEADS):
                r5 = R5[:, h * T:(h + 1) * T]
                bc = r5.rearrange("p (c j) -> p c j", c=NCH)
                if h:
                    dve.wait_ge(gstage_done, h)
                mid = bc[:, :, CH // 2 - 1:CH // 2].to_broadcast([P, NCH, CH])
                last = bc[:, :, CH - 1:CH].to_broadcast([P, NCH, CH])
                dve.tensor_tensor(EB[:, 0, :].rearrange("p (c j) -> p c j", c=NCH), bc, mid,
                                  ALU.subtract).then_inc(gdiff_ready, 1)
                dve.tensor_tensor(EB[:, 1, :].rearrange("p (c j) -> p c j", c=NCH), last, bc,
                                  ALU.subtract).then_inc(gdiff_ready, 1)
                dve.wait_ge(gexp_ready, 4 * h + 4)
                dve.tensor_copy(dec[:, h * NCH:(h + 1) * NCH], bc[:, :, CH - 1])
                dve.tensor_tensor(hT[:, h, :], qT[:, h, :], r5, ALU.mult)
                link(dve.tensor_tensor(hT[:, 4 + h, :], qT[:, 4 + h, :], EB[:, 1, :], ALU.mult))
                dve.tensor_tensor(qT[:, h, :], qT[:, h, :], atf, ALU.mult)
                dve.tensor_tensor(qT[:, 4 + h, :], qT[:, 4 + h, :], ssf, ALU.mult).then_inc(gstage_done, 1)
            dve.wait_ge(gstage_done, HEADS)
            link(dve.memset(AT[:, :, :], 0.0))

            def gla_norm(h):
                dve.wait_ge(*read(("gs", h)))
                link(dve.reciprocal(rrec, rstat))
                diagonals(rrec)
                dve.wait_ge(*full(("gb", h)))
                b = plan.at[("gb", h)][0]
                for j in range(2):
                    c = 2 * h + j
                    dve.wait_ge(*read(("gr", c)))
                    ins = dve.scalar_tensor_tensor(rG[:, c, :], rG[:, c, :], vcol("gla_norm_g", j), bank(b),
                                                   ALU.mult, ALU.mult)
                    if j == 0:
                        link(ins)
                    else:
                        ins.then_inc(bank_read[b], 1)
                dve.wait_ge(*read(("gb", h)))
                for j in range(2):
                    c = 2 * h + j
                    ob = plan.at[("go_ps", h, j)][0]
                    dve.tensor_tensor(rG[:, c, :], rG[:, c, :], bank(ob), ALU.mult).then_inc(bank_read[ob], 1)

            for h in range(HEADS):
                if h:
                    dve.wait_ge(*full(("go_ps", h - 1, 1)))
                dve.wait_ge(*full(("att", h)))
                b = plan.at[("att", h)][0]
                m = gmask[:, :].bitcast(U32).unsqueeze(1).to_broadcast([P, TT, P])
                dve.copy_predicated(AT[:, :, :], m, bank(b).rearrange("p (t i) -> p t i", t=TT)
                                    ).then_inc(bank_read[b], 1)
                if h:
                    gla_norm(h - 1)
                for c in range(1, NCH):
                    b = plan.at[("u", h, c - 1)][0]
                    kv = bank(b, 0, 256)
                    dve.wait_ge(*full(("u", h, c - 1)))
                    if c >= 3:
                        dve.wait_ge(inter_done, (NCH - 3) * h + c - 2)
                    if c == 1:
                        ins = dve.tensor_copy(SS[:, 1, :], kv)
                    else:
                        dve.wait_ge(*read(("u", h, c - 2)))
                        ins = dve.scalar_tensor_tensor(SS[:, c % 2, :], SS[:, (c - 1) % 2, :],
                                                       dec[:, h * NCH + c - 1:h * NCH + c], kv, ALU.mult, ALU.add)
                    ins.then_inc(bank_read[b], 1)
            gla_norm(HEADS - 1)
            residual(("go",))
            for c in range(C):
                dve.wait_ge(*read(("go", c)))
            attention(1)
            for c in range(C):
                dve.wait_ge(*read(("xo", 1, c)))
            moe(1)
            norm(LAST)
            for t in range(TT):
                evacuate(("out", t, 0), x_tm[:, t, 0:512])


_INS = ["x", "mem", "norm_mix", "norm_xattn", "norm_ffn", "norm_mem", "norm_final", "conv_w_in", "conv_b_in",
        "conv_w_dw", "conv_b_dw", "conv_ln_g", "conv_ln_b", "conv_w_out", "conv_b_out", "gla_w_in", "gla_w_a2",
        "gla_b_a", "gla_norm_g", "gla_w_o", "xa_w_q", "xa_w_kv", "xa_w_o", "moe_w_grp", "moe_b_grp", "moe_w_exp",
        "moe_b_exp", "moe_w_gate", "moe_w_up", "moe_w_down"]


def kernel(**inputs):
    import numpy as np
    import concourse.bacc as bacc
    from concourse.bass_utils import run_bass_kernel_spmd

    nc = bacc.Bacc("TRN2", target_bir_lowering=False, num_devices=1)
    arrays, args = {}, {}
    for name in _INS:
        arr = np.ascontiguousarray(inputs[name])
        arrays[f"in_{name}"] = arr
        args[name] = nc.dram_tensor(f"in_{name}", arr.shape, mybir.dt.from_np(arr.dtype), kind="ExternalInput").ap()
    out = nc.dram_tensor("out_0", (1, T, D), F32, kind="ExternalOutput").ap()
    build(nc, args, out)
    r = run_bass_kernel_spmd(nc, [arrays], core_ids=[0])
    return r.results[0]["out_0"]
```
